# Optimizing a Trainium2 kernel written in Bass

```python
import jax, jax.numpy as jnp
from jax import lax
import numpy as np

D_MODEL = 1024
BATCH = 1
SEQ = 256
DEPTH = 1
DEC_BATCH = 1
DEC_SEQ = 64
PAST_LEN = 512

CHUNK = 64
N_META = 16
Q_BLOCK = 128
M_HEADS = 4
M_DK = D_MODEL // M_HEADS
M_DV = D_MODEL // M_HEADS
M_QK = M_HEADS * M_DK
M_V = M_HEADS * M_DV
CONV_W = 4
A_HEADS = 8
NOPE_DIM = 128
ROPE_DIM = 64
V_HEAD = 128
Q_LORA = 3 * D_MODEL // 8
KV_LORA = D_MODEL // 4
ROPE_THETA = 10000.0
ATTN_SCALE = (NOPE_DIM + ROPE_DIM) ** -0.5
N_EXPERTS = 32
TOP_K = 4
D_FF = D_MODEL
SWIGLU_LIMIT = 7.0
SWIGLU_ALPHA = 1.702
MOE_BLOCK = 128
EPS = 1e-6
IN_SIZES = (2 * M_QK, M_V, M_V, M_HEADS, M_HEADS, Q_LORA, KV_LORA, ROPE_DIM, D_MODEL, D_MODEL)
IN_SPLITS = tuple(int(s) for s in np.cumsum(IN_SIZES)[:-1])
D_IN = int(sum(IN_SIZES))

kernel_name = 'hybrid_mlstm_mla_moe_stream_step'

def rmsnorm(x, g):
    xf = x.astype(jnp.float32)
    y = xf * lax.rsqrt(jnp.mean(xf * xf, axis=-1, keepdims=True) + EPS)
    return (y * g.astype(jnp.float32)).astype(x.dtype)

def rope(x, pos):
    half = x.shape[-1] // 2
    freqs = ROPE_THETA ** (-jnp.arange(half, dtype=jnp.float32) / half)
    ang = pos.astype(jnp.float32)[:, None] * freqs[None, :]
    shape = (ang.shape[0],) + (1,) * (x.ndim - 3) + (half,)
    cos = jnp.cos(ang).reshape(shape)
    sin = jnp.sin(ang).reshape(shape)
    xf = x.astype(jnp.float32)
    x1, x2 = xf[..., :half], xf[..., half:]
    return jnp.concatenate([x1 * cos - x2 * sin, x1 * sin + x2 * cos], axis=-1).astype(x.dtype)

def causal_conv(u, buf, w, b):
    xp = jnp.concatenate([buf.astype(u.dtype), u], axis=1)
    t = u.shape[1]
    out = b
    for j in range(CONV_W):
        out = out + xp[:, j:j + t] * w[j]
    return out, xp[:, xp.shape[1] - (CONV_W - 1):]

def mlstm_chunk(C, n, m, q, k, v, ig, lf):
    L = q.shape[1]
    b = jnp.swapaxes(jnp.cumsum(lf, axis=1), 1, 2)
    it = jnp.swapaxes(ig, 1, 2)
    causal = jnp.tril(jnp.ones((L, L), dtype=bool))
    d = jnp.where(causal, b[..., :, None] - b[..., None, :] + it[..., None, :], -jnp.inf)
    inter = b + m[..., None]
    m_t = jnp.maximum(inter, jnp.max(d, axis=-1))
    w_intra = jnp.exp(d - m_t[..., None])
    w_inter = jnp.exp(inter - m_t)
    s = jnp.einsum('blhd,bshd->bhls', q, k) * w_intra
    num = (jnp.einsum('bhls,bshe->blhe', s, v)
           + jnp.swapaxes(w_inter, 1, 2)[..., None] * jnp.einsum('blhd,bhde->blhe', q, C))
    qn = jnp.sum(s, axis=-1) + w_inter * jnp.einsum('blhd,bhd->bhl', q, n)
    den = jnp.maximum(jnp.abs(qn), jnp.exp(-m_t))
    h = num / jnp.swapaxes(den, 1, 2)[..., None]
    m_new = m_t[..., -1]
    w_prev = jnp.exp(b[..., -1] + m - m_new)
    w_k = jnp.exp(b[..., -1:] - b + it - m_new[..., None])
    C_new = w_prev[..., None, None] * C + jnp.einsum('bhs,bshd,bshe->bhde', w_k, k, v)
    n_new = w_prev[..., None] * n + jnp.einsum('bhs,bshd->bhd', w_k, k)
    return h, C_new, n_new, m_new

def mlstm_scan(C, n, m, q, k, v, ig, lf):
    B, T = q.shape[0], q.shape[1]
    nc = T // CHUNK

    def to_chunks(a):
        return jnp.moveaxis(a.reshape((B, nc, CHUNK) + a.shape[2:]), 1, 0)

    def step(carry, xs):
        h, C1, n1, m1 = mlstm_chunk(carry[0], carry[1], carry[2], *xs)
        return (C1, n1, m1), h

    (C, n, m), hs = lax.scan(step, (C, n, m), tuple(to_chunks(a) for a in (q, k, v, ig, lf)))
    h = jnp.moveaxis(hs, 0, 1).reshape((B, T) + hs.shape[3:])
    return h, C, n, m

def mla_attend(q_lat, q_rope, lat, kr, mask):
    s = (jnp.einsum('bqhr,bkr->bhqk', q_lat, lat)
         + jnp.einsum('bqhp,bkp->bhqk', q_rope, kr)).astype(jnp.float32) * ATTN_SCALE
    s = jnp.where(mask, s, -jnp.inf)
    p = jax.nn.softmax(s, axis=-1).astype(lat.dtype)
    return jnp.einsum('bhqk,bkr->bqhr', p, lat)

def moe(x2, w_router, b_router, w_gu, b_gu, w_dn, b_dn):
    M = x2.shape[0]
    logits = (x2 @ w_router).astype(jnp.float32) + b_router.astype(jnp.float32)
    top_v, top_i = lax.top_k(logits, TOP_K)
    gates = jax.nn.softmax(top_v, axis=-1)
    A = M * TOP_K
    flat_e = top_i.reshape(A)
    order = jnp.argsort(flat_e)
    se = flat_e[order]
    stok = order // TOP_K
    sgate = gates.reshape(A)[order]
    counts = jnp.zeros((N_EXPERTS,), jnp.int32).at[flat_e].add(1)
    pcounts = (counts + MOE_BLOCK - 1) // MOE_BLOCK * MOE_BLOCK
    start = jnp.cumsum(counts) - counts
    pend = jnp.cumsum(pcounts)
    pstart = pend - pcounts
    dest = pstart[se] + jnp.arange(A, dtype=jnp.int32) - start[se]
    n_blk = -(-A // MOE_BLOCK) + N_EXPERTS
    xs = jnp.zeros((n_blk * MOE_BLOCK, x2.shape[1]), x2.dtype).at[dest].set(x2[stok])
    blk_e = jnp.minimum(jnp.searchsorted(pend, jnp.arange(n_blk, dtype=jnp.int32) * MOE_BLOCK, side='right'),
                        N_EXPERTS - 1)

    def expert_block(args):
        xb, e = args
        gu = xb @ w_gu[e] + b_gu[e]
        gate = jnp.minimum(gu[:, :D_FF], SWIGLU_LIMIT)
        up = jnp.clip(gu[:, D_FF:], -SWIGLU_LIMIT, SWIGLU_LIMIT)
        hid = (up + 1.0) * gate * jax.nn.sigmoid(SWIGLU_ALPHA * gate)
        return hid @ w_dn[e] + b_dn[e]

    ys = lax.map(expert_block, (xs.reshape(n_blk, MOE_BLOCK, x2.shape[1]), blk_e))
    ys = ys.reshape(n_blk * MOE_BLOCK, x2.shape[1])
    return jnp.zeros_like(x2).at[stok].add(ys[dest] * sgate[:, None].astype(x2.dtype))

def trunk_layer(x, rope_pos, conv_buf, C0, n0, m0, lat_past, kr_past, prompt, lw):
    (g_mix, w_in, b_if, w_conv, b_conv, g_mh, w_proj_a, g_q, g_kv, w_uq, w_uk, w_uv, w_proj_b,
     w_out, g_ffn, w_router, b_router, w_gu, b_gu, w_dn, b_dn) = lw
    B, T, _ = x.shape
    z = rmsnorm(x, g_mix) @ w_in
    qk_pre, v_m, o_m, i_pre, f_pre, c_q, c_kv, k_r, g_a, g_b = jnp.split(z, IN_SPLITS, axis=-1)

    qk, new_buf = causal_conv(qk_pre, conv_buf, w_conv, b_conv)
    qk = jax.nn.silu(qk).astype(jnp.float32)
    q_m = qk[..., :M_QK].reshape(B, T, M_HEADS, M_DK)
    k_m = qk[..., M_QK:].reshape(B, T, M_HEADS, M_DK) * (M_DK ** -0.5)
    v_h = v_m.astype(jnp.float32).reshape(B, T, M_HEADS, M_DV)
    ig = i_pre.astype(jnp.float32) + b_if[:M_HEADS].astype(jnp.float32)
    lf = jax.nn.log_sigmoid(f_pre.astype(jnp.float32) + b_if[M_HEADS:].astype(jnp.float32))
    C0 = C0.astype(jnp.float32)
    n0 = n0.astype(jnp.float32)
    m0 = m0.astype(jnp.float32)
    if prompt:
        h0, C, n, m = mlstm_chunk(C0, n0, m0, q_m[:, :N_META], k_m[:, :N_META], v_h[:, :N_META],
                                  ig[:, :N_META], lf[:, :N_META])
        h1, C, n, m = mlstm_scan(C, n, m, q_m[:, N_META:], k_m[:, N_META:], v_h[:, N_META:],
                                 ig[:, N_META:], lf[:, N_META:])
        hm = jnp.concatenate([h0, h1], axis=1)
    else:
        hm, C, n, m = mlstm_chunk(C0, n0, m0, q_m, k_m, v_h, ig, lf)
    hm = hm * lax.rsqrt(jnp.mean(hm * hm, axis=-1, keepdims=True) + EPS)
    hm = (hm * g_mh.astype(jnp.float32).reshape(M_HEADS, M_DV)).reshape(B, T, M_V).astype(x.dtype)
    y_a = (hm * jax.nn.sigmoid(o_m)) @ w_proj_a

    q = (rmsnorm(c_q, g_q) @ w_uq).reshape(B, T, A_HEADS, NOPE_DIM + ROPE_DIM)
    q_nope = q[..., :NOPE_DIM]
    q_rope = rope(q[..., NOPE_DIM:], rope_pos)
    q_lat = jnp.einsum('bthn,rhn->bthr', q_nope, w_uk)
    lat = rmsnorm(c_kv, g_kv)
    kr = rope(k_r, rope_pos)
    if prompt:
        p = jnp.arange(T)
        kc = jnp.where(p < N_META, -1, (p - N_META) // CHUNK)
        o_meta = mla_attend(q_lat[:, :N_META], q_rope[:, :N_META], lat, kr,
                            jnp.broadcast_to(kc[None, :] < 0, (N_META, T)))
        nb = (T - N_META) // Q_BLOCK

        def blocks(a):
            return jnp.swapaxes(a[:, N_META:].reshape((B, nb, Q_BLOCK) + a.shape[2:]), 0, 1)

        def attend_block(args):
            ql, qr, bi = args
            qc = (bi * Q_BLOCK + jnp.arange(Q_BLOCK)) // CHUNK
            return mla_attend(ql, qr, lat, kr, kc[None, :] <= qc[:, None])

        o_fr = lax.map(attend_block, (blocks(q_lat), blocks(q_rope), jnp.arange(nb)))
        o_fr = jnp.swapaxes(o_fr, 0, 1).reshape(B, T - N_META, A_HEADS, KV_LORA)
        o_lat = jnp.concatenate([o_meta, o_fr], axis=1)
    else:
        keys_lat = jnp.concatenate([lat_past.astype(lat.dtype), lat], axis=1)
        keys_kr = jnp.concatenate([kr_past.astype(kr.dtype), kr], axis=1)
        o_lat = mla_attend(q_lat, q_rope, keys_lat, keys_kr, jnp.ones((T, keys_lat.shape[1]), dtype=bool))
    o_v = jnp.einsum('bthr,rhv->bthv', o_lat, w_uv).reshape(B, T, A_HEADS * V_HEAD)
    y_b = o_v @ w_proj_b

    mixed = jax.nn.sigmoid(g_a) * y_a + jax.nn.sigmoid(g_b) * y_b
    x = x + mixed @ w_out

    f = moe(rmsnorm(x, g_ffn).reshape(B * T, D_MODEL), w_router, b_router, w_gu, b_gu, w_dn, b_dn)
    x = x + f.reshape(B, T, D_MODEL)
    return x, (lat, kr, C, n, m, new_buf)

def setup_inputs(seed: int = 0) -> dict:
    key = jax.random.key(seed)
    ks = iter(jax.random.split(key, 40))

    def nrm(shape, scale):
        return jax.random.normal(next(ks), shape, jnp.float32) * scale

    def gain(shape):
        return 1.0 + nrm(shape, 0.01)

    b_if = jnp.concatenate([nrm((DEPTH, M_HEADS), 0.1),
                            jnp.linspace(3.0, 6.0, M_HEADS)[None, :] + nrm((DEPTH, M_HEADS), 0.1)], axis=-1)
    return {
        'x_prompt': nrm((BATCH, SEQ, D_MODEL), 1.0),
        'x_sample': nrm((DEC_BATCH, DEC_SEQ, D_MODEL), 1.0),
        'cache_kv_latent': nrm((DEPTH, DEC_BATCH, PAST_LEN, KV_LORA), 1.0),
        'cache_k_rope': nrm((DEPTH, DEC_BATCH, PAST_LEN, ROPE_DIM), 1.0),
        'state_mlstm_C': nrm((DEPTH, DEC_BATCH, M_HEADS, M_DK, M_DV), 0.02),
        'state_mlstm_n': nrm((DEPTH, DEC_BATCH, M_HEADS, M_DK), 0.1),
        'state_mlstm_m': nrm((DEPTH, DEC_BATCH, M_HEADS), 1.0),
        'state_conv': nrm((DEPTH, DEC_BATCH, CONV_W - 1, 2 * M_QK), 1.0),
        'meta_tokens': nrm((N_META, D_MODEL), 1.0),
        'g_mix_norm': gain((DEPTH, D_MODEL)),
        'w_in': nrm((DEPTH, D_MODEL, D_IN), D_MODEL ** -0.5),
        'b_if': b_if,
        'w_conv': nrm((DEPTH, CONV_W, 2 * M_QK), CONV_W ** -0.5),
        'b_conv': nrm((DEPTH, 2 * M_QK), 0.01),
        'g_mh_norm': gain((DEPTH, M_V)),
        'w_proj_a': nrm((DEPTH, M_V, D_MODEL), M_V ** -0.5),
        'g_q_norm': gain((DEPTH, Q_LORA)),
        'g_kv_norm': gain((DEPTH, KV_LORA)),
        'w_uq': nrm((DEPTH, Q_LORA, A_HEADS * (NOPE_DIM + ROPE_DIM)), Q_LORA ** -0.5),
        'w_uk': nrm((DEPTH, KV_LORA, A_HEADS, NOPE_DIM), KV_LORA ** -0.5),
        'w_uv': nrm((DEPTH, KV_LORA, A_HEADS, V_HEAD), KV_LORA ** -0.5),
        'w_proj_b': nrm((DEPTH, A_HEADS * V_HEAD, D_MODEL), (A_HEADS * V_HEAD) ** -0.5),
        'w_out': nrm((DEPTH, D_MODEL, D_MODEL), D_MODEL ** -0.5),
        'g_ffn_norm': gain((DEPTH, D_MODEL)),
        'w_router': nrm((DEPTH, D_MODEL, N_EXPERTS), D_MODEL ** -0.5),
        'b_router': nrm((DEPTH, N_EXPERTS), 0.01),
        'w_gate_up': nrm((DEPTH, N_EXPERTS, D_MODEL, 2 * D_FF), D_MODEL ** -0.5),
        'b_gate_up': nrm((DEPTH, N_EXPERTS, 2 * D_FF), 0.01),
        'w_down': nrm((DEPTH, N_EXPERTS, D_FF, D_MODEL), D_FF ** -0.5),
        'b_down': nrm((DEPTH, N_EXPERTS, D_MODEL), 0.01),
        'g_final_norm': gain((D_MODEL,)),
    }

def reference(x_prompt, x_sample, cache_kv_latent, cache_k_rope, state_mlstm_C, state_mlstm_n, state_mlstm_m,
              state_conv, meta_tokens, g_mix_norm, w_in, b_if, w_conv, b_conv, g_mh_norm, w_proj_a, g_q_norm,
              g_kv_norm, w_uq, w_uk, w_uv, w_proj_b, w_out, g_ffn_norm, w_router, b_router, w_gate_up, b_gate_up,
              w_down, b_down, g_final_norm):
    B, S = x_prompt.shape[0], x_prompt.shape[1]
    DB, DS = x_sample.shape[0], x_sample.shape[1]
    PL = cache_kv_latent.shape[2]
    xp = jnp.concatenate([jnp.broadcast_to(meta_tokens.astype(x_prompt.dtype)[None], (B, N_META, D_MODEL)),
                          x_prompt], axis=1)
    pos_p = jnp.arange(N_META + S)
    pos_s = N_META + PL + jnp.arange(DS)
    xs = x_sample
    p_states = []
    s_states = []
    for l in range(DEPTH):
        lw = (g_mix_norm[l], w_in[l], b_if[l], w_conv[l], b_conv[l], g_mh_norm[l], w_proj_a[l], g_q_norm[l],
              g_kv_norm[l], w_uq[l], w_uk[l], w_uv[l], w_proj_b[l], w_out[l], g_ffn_norm[l], w_router[l],
              b_router[l], w_gate_up[l], b_gate_up[l], w_down[l], b_down[l])
        xp, ps = trunk_layer(xp, pos_p, jnp.zeros((B, CONV_W - 1, 2 * M_QK), xp.dtype),
                             jnp.zeros((B, M_HEADS, M_DK, M_DV), jnp.float32),
                             jnp.zeros((B, M_HEADS, M_DK), jnp.float32),
                             jnp.zeros((B, M_HEADS), jnp.float32), None, None, True, lw)
        xs, ss = trunk_layer(xs, pos_s, state_conv[l], state_mlstm_C[l], state_mlstm_n[l], state_mlstm_m[l],
                             cache_kv_latent[l], cache_k_rope[l], False, lw)
        p_states.append(ps)
        s_states.append(ss)
    p_lat = jnp.stack([st[0] for st in p_states])
    p_kr = jnp.stack([st[1] for st in p_states])
    p_C = jnp.stack([st[2] for st in p_states])
    p_n = jnp.stack([st[3] for st in p_states])
    p_m = jnp.stack([st[4] for st in p_states])
    p_conv = jnp.stack([st[5] for st in p_states])
    s_lat = jnp.stack([st[0] for st in s_states])
    s_kr = jnp.stack([st[1] for st in s_states])
    s_C = jnp.stack([st[2] for st in s_states])
    s_n = jnp.stack([st[3] for st in s_states])
    s_m = jnp.stack([st[4] for st in s_states])
    s_conv = jnp.stack([st[5] for st in s_states])
    y_prompt = rmsnorm(xp[:, N_META:], g_final_norm)
    y_sample = rmsnorm(xs, g_final_norm)
    return (y_prompt, y_sample, p_lat, p_kr, p_C, p_n, p_m, p_conv, s_lat, s_kr, s_C, s_n, s_m, s_conv)


_drawn_inputs = setup_inputs


def setup_inputs(seed=0):
    import zlib

    import numpy as np

    out = dict(_drawn_inputs(seed))
    spreads = {}
    factors = {'state_mlstm_m': 3.537,
     'b_conv': 2.704,
     'g_mh_norm': 23.921,
     'g_q_norm': 6.674,
     'g_kv_norm': 4.318,
     'b_gate_up': 24.776,
     'b_down': 86.053,
     'g_final_norm': 194.046,
     'cache_kv_latent': 8.0,
     'cache_k_rope': 8.0,
     'g_ffn_norm': 4.466,
     'b_router': 12.244}
    for name, (base, spread) in spreads.items():
        noise = np.random.default_rng([zlib.crc32(name.encode()), seed]).standard_normal(out[name].shape)
        drawn = base * np.exp(spread * noise) if base else spread * noise
        out[name] = __import__('jax').numpy.asarray(drawn.astype(out[name].dtype))
    for name, factor in factors.items():
        out[name] = (out[name] * factor).astype(out[name].dtype)
    return out
```

```python
import concourse.bass as bass
import numpy as np
from concourse import mybir
from contextlib import ExitStack

F32 = mybir.dt.float32
I32 = mybir.dt.int32
U32 = mybir.dt.uint32
ALU = mybir.AluOpType
ACT = mybir.ActivationFunctionType
AX = mybir.AxisListType

D = 1024
KD = D // 128
TS, TM, TX = 64, 16, 256
TP = TM + TX
NT = TS + TP
PAST = 512
ROWS = [(0, 128), (128, 128), (256, NT - 256)]
CHUNKS = [(0, 64), (64, 16)] + [(80 + 64 * c, 64) for c in range(4)]
KEYS = [(64, 128), (192, 128), (320, 16), (0, 64)]
MH, AH = 4, 8
NOPE, ROPE, KVL, QL = 128, 64, 256, 384
NE, TOPK, BLK = 32, 4, 64
MAXB = NE + NT * TOPK // BLK
NB1 = MAXB + 2
SCALE = float(np.float32((NOPE + ROPE) ** -0.5))
EPS = 1e-6
LIMIT, ALPHA = 7.0, 1.702
NEG = -1e30

CONST_AT = {}
_at = 0
for _name, _n in [("ident", 128), ("ones", 128), ("below", 128), ("cos", NT), ("sin", NT), ("swap", 64),
                  ("mask", NT), ("sel", 4 * 128), ("expert", NE), ("block", NB1), ("slot", BLK)]:
    CONST_AT[_name] = (_at, _n)
    _at += _n
CONST_N = _at


def constants():
    c = np.zeros((128, CONST_N), np.float32)

    def put(name, a):
        o, n = CONST_AT[name]
        c[:a.shape[0], o:o + n] = a

    put("ident", np.eye(128))
    put("ones", np.ones((128, 128)))
    put("below", np.triu(np.ones((128, 128)), 1))
    half = ROPE // 2
    pos = np.concatenate([TM + PAST + np.arange(TS), np.arange(TP)]).astype(np.float32)
    freq = np.float32(10000.0) ** (-np.arange(half, dtype=np.float32) / np.float32(half))
    ang = (pos[None, :] * freq[:, None].astype(np.float32)).astype(np.float32)
    put("cos", np.concatenate([np.cos(ang), np.cos(ang)]))
    put("sin", np.concatenate([-np.sin(ang), np.sin(ang)]))
    put("swap", np.roll(np.eye(ROPE), half, axis=0))
    mask = np.zeros((64, NT))
    for c0, n in CHUNKS:
        mask[:, c0:c0 + n] = np.where(np.arange(64)[:, None] <= np.arange(n)[None, :], 0.0, NEG)
    put("mask", mask)
    sel = np.zeros((4, 4, 128))
    for h in range(4):
        sel[h, h] = 1
    put("sel", sel.reshape(4, 512))
    put("expert", np.tile(np.arange(NE), (128, 1)))
    put("block", np.tile(np.arange(NB1), (128, 1)))
    put("slot", np.tile(np.arange(BLK), (128, 1)))
    return c


PANELS = (["ifq", "kv"] + [f"qk{i}" for i in range(4)] + ["v0", "v1", "o0", "o1", "uq0", "uq1", "ukuv"]
          + [f"g{i}" for i in range(4)] + ["pa0", "pa1", "pb0", "pb1", "wo0", "wo1"])
SLOT = 4096
UPSLOT, DNSLOT = [4, 5, 3, 0], [1, 2]


def by_chunk(pair, h, src):
    return [(pair[:, TS * h:TS * h + TS], src[:, 0:TS]),
            (pair[:, 2 * TS + TM * h:2 * TS + TM * h + TM], src[:, TS:TS + TM]),
            (pair[:, 2 * (TS + TM):2 * NT].rearrange("p (c h t) -> p c h t", c=4, h=2)[:, :, h, :],
             src[:, TS + TM:NT].rearrange("p (c t) -> p c t", c=4))]


def units(hp):
    return [(hp, c) for c in range(6)]


def job_list():
    j = [("vecT",), ("convT",), ("buT",), ("bdT",)]
    j += [("xT", t, s) for t in range(3) for s in range(2)]
    j += [("ig",), ("fg",)] + [("cq", i) for i in range(3)]
    j += [("ckv", 0), ("ckv", 1), ("kr",), ("ssq",), ("ssk",), ("krs",)]
    j += [("qk", i) for i in range(8)]
    j += [("kvrow", t) for t in range(4)]
    j += [("qk", i) for i in range(8, 16)]
    j += [("wi", h) for h in range(4)] + [("mx", h) for h in range(4)] + [("cols",)]
    j += [("v", i) for i in range(8)] + [("convrow",)]
    j += [("o", i) for i in range(8)]
    for c in range(6):
        j += [("krow", c, s) for s in range(2)] + [("vrow", c, s) for s in range(2)] + [("s", c)]
        j += [("num", c, h) for h in range(4)]
        j += [("upd", c, i) for i in range(8)]
        if c in (0, 5):
            j += [("nT", c)]
        if c:
            j += [("hT", c - 1)]
    j += [("hT", 5)]
    j += [("cacheT", t) for t in range(4)]
    for hp in range(4):
        j += [("ukT", hp)]
        for h in (0, 1):
            j += [("qn", hp, h), ("qr", hp, h), ("qrs", hp, h)]
        j += [("ql", hp, i) for i in range(4)]
        u = units(hp)
        for n in range(len(u) + 1):
            if n < len(u):
                j += [("sc",) + u[n] + (p,) for p in range(2 if u[n][1] == 0 else 1)]
            if n:
                j += [("pT",) + u[n - 1] + (p,) for p in range(2 if u[n - 1][1] == 0 else 1)]
                j += [("ol",) + u[n - 1]]
        j += [("ov", hp, h) for h in (0, 1)]
    j += [("g", i) for i in range(16)]
    j += [("ya", i) for i in range(8)] + [("yb", i) for i in range(8)]
    j += [("out", t, s) for t in range(3) for s in range(2)]
    j += [("x2T", t, s) for t in range(3) for s in range(2)]
    j += [("lg", t) for t in range(3)] + [("pos", t) for t in range(3)] + [("cnt",)]
    return j


JOBS = job_list()
JOB = {name: n for n, name in enumerate(JOBS)}
assert len(JOB) == len(JOBS)


def qcol(col):
    return col if col < TS else col + 3


def build(nc, i, o, y_rows_dram):
    with ExitStack() as ctx:
        def sb(name, shape, dt=F32):
            return ctx.enter_context(nc.sbuf_tensor(name, shape, dt))

        def sem(name):
            return ctx.enter_context(nc.semaphore(name))

        ring = sb("ring", [128, 6 * SLOT])
        r_xt = sb("r_xt", [128, KD * NT])
        r_o = sb("r_o", [128, KD * NT])
        r_kv = sb("r_kv", [128, 3968])
        r_qk = sb("r_qk", [128, 16 * (NT + 3)])
        r_v = sb("r_v", [128, KD * NT])
        r_c = sb("r_c", [128, 4112])
        const = sb("const", [128, CONST_N])
        bu_t = sb("bu_t", [128, 16, NE])
        bd_t = sb("bd_t", [128, 8, NE])
        vec_rows = sb("vec_rows", [128, 128])
        conv_rows = sb("conv_rows", [48, 128])
        vec = sb("vec", [128, 112])
        convst = sb("convst", [128, 3, 16])
        b_router_b = sb("b_router_b", [128, NE])
        u_pad = sb("u_pad", [128, 2, NT + 6])
        sig = sb("sig", [128, 2, NT + 3])
        tail = sb("tail", [128, 2, 3, 16])
        tailrow = sb("tailrow", [96, 128])
        ss = sb("ss", [128, 16])
        b_if = sb("b_if", [4, 2])
        mst = sb("mst", [4, 16])
        wprev = sb("wprev", [128, 4, 6])
        colT = sb("colT", [64, 6, 3, 4])
        hs = sb("hs", [64, 8, 4])
        nrow = sb("nrow", [8, 2, 128])
        st = sb("st", [128, 2, 8])

        def cst(name, rows=128):
            at, n = CONST_AT[name]
            return const[0:rows, at:at + n]

        def r3(ap, a):
            return ap.rearrange("p (a b) -> p a b", a=a)

        ident = cst("ident")
        scratch = ring[:, 4 * SLOT:6 * SLOT]

        x_rows = r3(scratch[:, 0:3072], 3)
        xn_rows = r3(scratch[:, 3072:6144], 3)
        bu_rows = r_qk[0:NE, 0:2048]
        bd_rows = r_qk[0:NE, 2048:3072]
        xT = r3(r_xt[:, :], KD)
        qk = r3(r_qk[:, :], 16)
        vT = r3(r_v[:, :], KD)
        oT = r3(r_o[:, :], KD)
        cq = r3(r_kv[:, 0:1008], 3)
        lat = r3(r_kv[:, 1008:1680], 2)
        krT = r_kv[0:64, 1680:2016]
        kvrow = r3(r_kv[:, 2016:3296], 4)
        rq = r_kv[:, 3296:3632]
        rk = r_kv[:, 3632:3968]
        sq = r3(r_v[:, 0:5 * NT], 5)
        kr_raw = r_v[0:64, 5 * NT:6 * NT]
        kr_tmp = r_v[0:64, 6 * NT:7 * NT]
        rows4 = r3(r_o[0:4, :], 8)
        R_IG, R_LF, R_B, R_A, R_MX, R_WI, R_DN, R_WK = (rows4[:, n, :] for n in range(8))
        krow = r3(scratch[0:64, 0:2048], 2)
        vrow = r3(scratch[0:64, 2048:4104], 2)
        emat = r3(scratch[0:64, 4104:5448], 4)
        wib = r3(scratch[:, 5448:6792], 4)
        sT = r3(scratch[0:64, 6792:7048], 4)
        junk = scratch[0:64, 7048:7304]
        wexp = r3(scratch[0:64, 7304:7560], 4)
        C = r3(r_c[:, 0:2056], 8)
        num = r_c[0:64, 2056:4112].rearrange("p (b h e) -> p b h e", b=2, h=4)
        qn = r3(scratch[:, 0:672], 2)
        qlat = r3(scratch[:, 672:2016], 2)
        qr = scratch[0:64, 2016:2688]
        qx = r3(scratch[0:64, 2688:3360], 2)
        olat = scratch[:, 3360:4704].rearrange("p (r h t) -> p r h t", r=2, h=2)
        prob = r3(scratch[:, 4704:5856], 2)
        pT = scratch[:, 5856:7136].rearrange("p (b k q) -> p b k q", b=2, k=5)
        ukT = scratch[:, 7136:7648].rearrange("p (h r) -> p h r", h=2)
        qtmp = scratch[0:64, 7648:7984]
        cache_row = r3(r_c[:, 0:1280], 4)
        cache_lat = r3(r_c[:, 1280:2304], 2)
        cache_kr = r_c[0:64, 2304:2816]
        ovT = r3(r_v[:, :], KD)
        gates = r3(r_qk[:, 0:16 * NT], 16)
        mixed = r3(r_xt[:, :], KD)
        x1 = r3(r_c[:, 0:3072], 3)
        x2 = r3(r_qk[:, 0:3072], 3)
        x2T = r3(r_o[:, :], KD)
        g_ffn_b = r_v[:, 1216:2240]
        g_fin_b = r_xt[:, 0:1024]
        w_rt = r3(r_xt[:, 1024:1280], KD)

        tab_at = [3072]

        def small(n, rows=128):
            a = tab_at[0]
            tab_at[0] += n
            assert tab_at[0] <= 16 * (NT + 3)
            return r_qk[0:rows, a:a + n]

        logit = r3(small(3 * NE), 3)
        top = r3(small(24), 3)
        topi = r3(small(24), 3)
        topif = r3(small(24), 3)
        onehot = small(12 * NE).rearrange("p (t k e) -> p t k e", t=3, k=4)
        chosen = r3(small(3 * NE), 3)
        gate = r3(small(24), 3)
        gsum = small(8)
        posm = r3(small(3 * NE), 3)
        dest = r3(small(12), 3)
        desti = r3(small(12), 3)
        loc = r3(small(3 * NB1), 3)
        t1 = small(NB1)
        t2 = small(NB1)
        nblk = small(NE)
        pend = small(NE)
        start = small(NE)
        t32 = small(NE)
        be = small(NB1)
        bei = small(NB1)
        nbi = small(2)

        xg = r3(r_kv[:, 0:512], 8)
        gt = r3(r_kv[:, 512:1024], 8)
        up = r3(r_kv[:, 1024:1536], 8)
        sg = r3(r_kv[:, 1536:2048], 8)
        hid = r3(r_kv[:, 2048:2560], 8)
        yT = r3(r_kv[:, 2560:3072], 8)
        yrow = r_v[0:BLK, 0:1024]
        pick = r3(r_v[:, 1024:1216], 3)

        def up_w(c):
            return ring[:, UPSLOT[c] * SLOT:(UPSLOT[c] + 1) * SLOT].rearrange("p (k f) -> p k f", k=2)

        def dn_w(c):
            return ring[:, DNSLOT[c] * SLOT:(DNSLOT[c] + 1) * SLOT].rearrange("p (k f) -> p k f", k=4)

        V_GMIX, V_BCONV, V_WCONV, V_GMH, V_GQ, V_GKV, V_N0 = 0, 8, 24, 88, 96, 99, 101
        NVEC = 109

        banks = [ctx.enter_context(nc.psum_tensor(f"bank{b}", [128, 512], F32)) for b in range(8)]
        bank_full = [sem(f"bank_full{b}") for b in range(8)]
        bank_free = [sem(f"bank_free{b}") for b in range(8)]

        def bank(name):
            return banks[JOB[name] % 8]

        def filled(eng, *name):
            n = JOB[name]
            eng.wait_ge(bank_full[n % 8], n // 8 + 1)

        def taken(eng, *name):
            n = JOB[name]
            eng.wait_ge(bank_free[n % 8], n // 8 + 1)

        ld_const, ld_vec, ld_x, ld_mem, ld_be, ld_late = map(sem, (
            "ld_const", "ld_vec", "ld_x", "ld_mem", "ld_be", "ld_late"))
        ld_cache, ld_x1 = sem("ld_cache"), sem("ld_x1")
        slot_in = [sem(f"slot_in{n}") for n in range(4)]
        chunk_in = [sem(f"chunk_in{n}") for n in range(6)]
        (rms_v, rms_s, xn_ready, cq_ready, kv_ready, kr_ready, low_v, low_s, conv_done, sig_ready, qk_ready,
         tail_done, pad_set, ones_set, n_set, lg_d, lg_a, gates_x, gates4, wprev_ready, e_ready, q_scaled, hs_v, hs_s,
         hn_ready, q_ready, pmax, pnorm, mix_a, x1_ss, x1_v, x1_s, x2_ready, chosen_set, gate_x, gate_e, moe_tab,
         stored, stored_c) = map(sem, (
             "rms_v", "rms_s", "xn_ready", "cq_ready", "kv_ready", "kr_ready", "low_v", "low_s", "conv_done",
             "sig_ready", "qk_ready", "tail_done", "pad_set", "ones_set", "n_set", "lg_d", "lg_a", "gates_x", "gates4",
             "wprev_ready", "e_ready", "q_scaled", "hs_v", "hs_s", "hn_ready", "q_ready", "pmax", "pnorm", "mix_a",
             "x1_ss", "x1_v", "x1_s", "x2_ready", "chosen_set", "gate_x", "gate_e", "moe_tab", "stored", "stored_c"))
        (m_pick, m_gath, m_xg, m_gt, m_sig, m_hid, m_yt, m_tr, m_yrow, m_used, m_store, m_dve, m_act,
         fin_v, fin_ss, fin_s, fin_out, all_out) = map(sem, (
             "m_pick", "m_gath", "m_xg", "m_gt", "m_sig", "m_hid", "m_yt", "m_tr", "m_yrow", "m_used", "m_store",
             "m_dve", "m_act", "fin_v", "fin_ss", "fin_s", "fin_out", "all_out"))
        desti_set, blocks_out = sem("desti_set"), sem("blocks_out")
        yrow_free, zero_set, rows_zeroed = sem("yrow_free"), sem("zero_set"), sem("rows_zeroed")
        fin_y = [sem(f"fin_y{t}") for t in range(3)]
        dve_step, act_step = sem("dve_step"), sem("act_step")

        def pslot(p, n):
            return ring[:, (p % 4) * SLOT:(p % 4) * SLOT + n]

        w_in = i["w_in"][0].rearrange("(k p) c -> p k c", p=128)
        sq_w = {n: i[w][0].rearrange("(k p) c -> p k c", p=128)
                for n, w in (("pa", "w_proj_a"), ("pb", "w_proj_b"), ("wo", "w_out"))}
        in_at = {"ifq": (4096, 392), "kv": (4488, 320)}
        for n in range(4):
            in_at[f"qk{n}"] = (512 * n, 512)
            in_at[f"g{n}"] = (4808 + 512 * n, 512)
        for n in range(2):
            in_at[f"v{n}"] = (2048 + 512 * n, 512)
            in_at[f"o{n}"] = (3072 + 512 * n, 512)
        PV, loads, need = {}, {}, {}
        slot_sum = [0] * 4
        for p, name in enumerate(PANELS):
            if name in in_at:
                at, n = in_at[name]
                PV[name] = r3(pslot(p, 8 * n), 8)
                loads[name] = [(PV[name], w_in[:, :, at:at + n])]
            elif name[:2] in sq_w:
                PV[name] = r3(pslot(p, 4096), 8)
                c = int(name[2])
                loads[name] = [(PV[name], sq_w[name[:2]][:, :, 512 * c:512 * c + 512])]
            elif name[:2] == "uq":
                PV[name] = r3(pslot(p, 3 * 768), 3)
                c = int(name[2])
                loads[name] = [(PV[name], i["w_uq"][0].rearrange("(k p) c -> p k c", p=128)[
                    :, :, 768 * c:768 * c + 768])]
            else:
                v = pslot(p, 4096)
                PV["uk"], PV["uv"] = r3(v[:, 0:2048], 2), r3(v[:, 2048:4096], 2)
                loads[name] = [(PV[w], i["w_" + w][0].rearrange("(k p) h n -> p k (h n)", p=128))
                               for w in ("uk", "uv")]
            slot_sum[p % 4] += 16 * len(loads[name])
            need[name] = slot_sum[p % 4]
        last_job = {"ifq": ("cq", 2), "kv": ("kr",), "uq0": ("qr", 1, 1), "uq1": ("qr", 3, 1), "ukuv": ("ov", 3, 1)}
        for n in range(4):
            last_job[f"qk{n}"] = ("qk", 4 * n + 3)
            last_job[f"g{n}"] = ("g", 4 * n + 3)
        for n in range(2):
            last_job[f"v{n}"] = ("v", 4 * n + 3)
            last_job[f"o{n}"] = ("o", 4 * n + 3)
            last_job[f"pa{n}"] = ("ya", 4 * n + 3)
            last_job[f"pb{n}"] = ("yb", 4 * n + 3)
            last_job[f"wo{n}"] = ("out", 2, n)

        def panel_here(eng, name):
            eng.wait_ge(slot_in[PANELS.index(name) % 4], need[name])

        gu = i["w_gate_up"][0].rearrange("e (k p) f -> p e k f", p=128)
        dn = i["w_down"][0].rearrange("e (k p) f -> p e k f", p=128)

        block = ctx.enter_context(nc.Block())

        @block.sync
        def _(sp):
            sp.dma_start(x_rows[0:64, 0, :], i["x_sample"][0]).then_inc(ld_x, 16)
            sp.dma_start(x_rows[64:80, 0, :], i["meta_tokens"]).then_inc(ld_x, 16)
            sp.dma_start(x_rows[80:128, 0, :], i["x_prompt"][0, 0:48, :]).then_inc(ld_x, 16)
            sp.dma_start(x_rows[:, 1, :], i["x_prompt"][0, 48:176, :]).then_inc(ld_x, 16)
            sp.dma_start(x_rows[0:80, 2, :], i["x_prompt"][0, 176:256, :]).then_inc(ld_x, 16)
            sp.dma_start(const[:, :], i["consts"]).then_inc(ld_const, 16)
            at = 0
            for name, n in (("g_mix_norm", 8), ("b_conv", 16), ("w_conv", 64), ("g_mh_norm", 8), ("g_q_norm", 3),
                            ("g_kv_norm", 2), ("state_mlstm_n", 8)):
                flat = i[name].rearrange({2: "a b -> (a b)", 3: "a b c -> (a b c)", 4: "a b c d -> (a b c d)"}[
                    len(i[name].shape)])
                sp.dma_start(vec_rows[at:at + n, :], flat.rearrange("(a b) -> a b", b=128)).then_inc(ld_vec, 16)
                at += n
            sp.dma_start(conv_rows[:, :], i["state_conv"].rearrange("a b j (c p) -> (a b j c) p", p=128)
                         ).then_inc(ld_vec, 16)
            sp.dma_start(bu_rows, i["b_gate_up"][0]).then_inc(ld_vec, 16)
            sp.dma_start(bd_rows, i["b_down"][0]).then_inc(ld_vec, 16)
            for n in range(4):
                for dst, src in loads[PANELS[n]]:
                    sp.dma_start(dst, src).then_inc(slot_in[n], 16)
            sp.dma_start(b_if[:, :], i["b_if"].rearrange("a (j h) -> h (a j)", h=4),
                         allow_slow_non_contiguous=True).then_inc(ld_mem, 16)
            sp.dma_start(mst[:, 0:1], i["state_mlstm_m"].rearrange("a b h -> h (a b)"),
                         allow_slow_non_contiguous=True).then_inc(ld_mem, 16)
            sp.dma_start(C[:, :, 0:256], i["state_mlstm_C"][0, 0].rearrange("h (b p) e -> p (h b) e", p=128)
                         ).then_inc(ld_mem, 16)
            sp.dma_start(b_router_b[:, :], i["b_router"].broadcast_to([128, NE])).then_inc(ld_mem, 16)
            for p in range(4, len(PANELS)):
                filled(sp, *last_job[PANELS[p - 4]])
                for dst, src in loads[PANELS[p]]:
                    sp.dma_start(dst, src).then_inc(slot_in[p % 4], 16)
                if PANELS[p] == "g0":
                    sp.wait_ge(stored_c, 32)
                    filled(sp, "hT", 5)
                    sp.dma_start(cache_row[:, :, 0:256], i["cache_kv_latent"][0, 0].rearrange("(t p) r -> p t r", p=128)
                                 ).then_inc(ld_cache, 16)
                    sp.dma_start(cache_row[:, :, 256:320], i["cache_k_rope"][0, 0].rearrange("(t p) r -> p t r", p=128)
                                 ).then_inc(ld_cache, 16)
            filled(sp, "ov", 3, 1)
            sp.dma_start(x1[0:64, 0, :], i["x_sample"][0]).then_inc(ld_x1, 16)
            sp.dma_start(x1[64:80, 0, :], i["meta_tokens"]).then_inc(ld_x1, 16)
            sp.dma_start(x1[80:128, 0, :], i["x_prompt"][0, 0:48, :]).then_inc(ld_x1, 16)
            sp.dma_start(x1[:, 1, :], i["x_prompt"][0, 48:176, :]).then_inc(ld_x1, 16)
            sp.dma_start(x1[0:80, 2, :], i["x_prompt"][0, 176:256, :]).then_inc(ld_x1, 16)
            sp.dma_start(up_w(0), gu[:, 0, 0:2, :]).then_inc(chunk_in[0], 16)
            sp.dma_start(up_w(1), gu[:, 0, 2:4, :]).then_inc(chunk_in[1], 16)
            filled(sp, "yb", 7)
            sp.dma_start(g_ffn_b, i["g_ffn_norm"].broadcast_to([128, D])).then_inc(ld_late, 16)
            sp.dma_start(up_w(2), gu[:, 0, 4:6, :]).then_inc(chunk_in[2], 16)
            sp.dma_start(up_w(3), gu[:, 0, 6:8, :]).then_inc(chunk_in[3], 16)
            filled(sp, "out", 2, 0)
            filled(sp, "out", 2, 1)
            sp.dma_start(w_rt, i["w_router"][0].rearrange("(k p) e -> p k e", p=128)).then_inc(ld_late, 16)
            sp.dma_start(g_fin_b, i["g_final_norm"].rearrange("(a d) -> a d", a=1).broadcast_to([128, D])
                         ).then_inc(ld_late, 16)
            sp.dma_start(dn_w(0), dn[:, 0, 0:4, :]).then_inc(chunk_in[4], 16)
            sp.dma_start(dn_w(1), dn[:, 0, 4:8, :]).then_inc(chunk_in[5], 16)
            sp.wait_ge(moe_tab, 1)
            nb = sp.value_load(nbi[0:1, 0:1].bitcast(I32), min_val=NE, max_val=MAXB)
            with sp.Fori(1, nb) as b:
                e = sp.value_load(bei[0:1, bass.ds(b, 1)].bitcast(I32), min_val=0, max_val=NE - 1)
                for c in range(6):
                    dst = up_w(c) if c < 4 else dn_w(c - 4)
                    src = gu[:, bass.ds(e, 1), 2 * c:2 * c + 2, :] if c < 4 else \
                        dn[:, bass.ds(e, 1), 4 * (c - 4):4 * (c - 4) + 4, :]
                    sp.wait_ge(m_used, (b - 1) * 6 + c + 1)
                    sp.dma_start(dst, src.rearrange("p a k f -> p (a k) f")).then_inc(chunk_in[c], 16)

        @block.tensor
        def _(pe):
            def begin(*name):
                n = JOB[name]
                if n >= 8:
                    pe.wait_ge(bank_free[n % 8], n // 8)
                return banks[n % 8]

            def end(ins, *name):
                ins.then_inc(bank_full[JOB[name] % 8], 1)

            def group(out, pairs, **kw):
                for n, (l, r) in enumerate(pairs):
                    ins = pe.matmul(out, l, r, start=(n == 0), stop=(n == len(pairs) - 1), **kw)
                return ins

            def turn(out, src):
                return pe.transpose(out, src, ident[0:src.shape[0], 0:src.shape[0]])

            pe.wait_ge(ld_const, 16)
            pe.wait_ge(ld_vec, 160)
            b = begin("vecT")
            end(turn(b[:, 0:NVEC], vec_rows[0:NVEC, :]), "vecT")
            b = begin("convT")
            end(turn(b[:, 0:48], conv_rows[:, :]), "convT")
            b = begin("buT")
            for n in range(16):
                ins = turn(b[:, 32 * n:32 * n + 32], bu_rows[:, 128 * n:128 * n + 128])
            end(ins, "buT")
            b = begin("bdT")
            for n in range(8):
                ins = turn(b[:, 32 * n:32 * n + 32], bd_rows[:, 128 * n:128 * n + 128])
            end(ins, "bdT")
            for t, (c0, n) in enumerate(ROWS):
                pe.wait_ge(xn_ready, t + 1)
                for s in range(2):
                    b = begin("xT", t, s)
                    for k in range(4):
                        ins = turn(b[:, n * k:n * k + n], xn_rows[0:n, t, 128 * (4 * s + k):128 * (4 * s + k) + 128])
                    end(ins, "xT", t, s)

            def project(name, panel, at, m, src=xT, kk=KD):
                b = begin(*name)
                end(group(b[0:m, 0:NT], [(PV[panel][:, k, at:at + m], src[:, k, :]) for k in range(kk)]), *name)

            for t in range(3):
                for s in range(2):
                    taken(pe, "xT", t, s)
            panel_here(pe, "ifq")
            project(("ig",), "ifq", 0, 4)
            project(("fg",), "ifq", 4, 4)
            for n in range(3):
                project(("cq", n), "ifq", 8 + 128 * n, 128)
            panel_here(pe, "kv")
            for n in range(2):
                project(("ckv", n), "kv", 128 * n, 128)
            project(("kr",), "kv", 256, 64)
            for name, lo, hi in (("ssq", 0, 3), ("ssk", 3, 5)):
                pe.wait_ge(cq_ready, hi)
                b = begin(name)
                end(group(b[:, 0:NT], [(cst("ones"), sq[:, k, :]) for k in range(lo, hi)]), name)
            taken(pe, "kr")
            b = begin("krs")
            end(group(b[0:64, 0:NT], [(cst("swap", 64), kr_raw)]), "krs")
            for n in range(16):
                if n == 8:
                    pe.wait_ge(kv_ready, 2)
                    pe.wait_ge(kr_ready, 1)
                    for t, (c0, m) in enumerate(KEYS):
                        b = begin("kvrow", t)
                        turn(b[0:m, 0:128], lat[:, 0, c0:c0 + m])
                        turn(b[0:m, 128:256], lat[:, 1, c0:c0 + m])
                        end(turn(b[0:m, 256:320], krT[:, c0:c0 + m]), "kvrow", t)
                panel_here(pe, f"qk{n // 4}")
                project(("qk", n), f"qk{n // 4}", 128 * (n % 4), 128)
            pe.wait_ge(gates4, 1)
            for h in range(4):
                b = begin("wi", h)
                end(group(b[:, 0:NT], [(cst("sel", 4)[:, 128 * h:128 * h + 128], R_WI)]), "wi", h)
            for h in range(4):
                b = begin("mx", h)
                end(group(b[0:64, 0:NT], [(cst("sel", 4)[:, 128 * h:128 * h + 64], R_MX)]), "mx", h)
            b = begin("cols")
            for c, (c0, m) in enumerate(CHUNKS):
                for q, row in enumerate((R_A, R_DN, R_WK)):
                    at = 12 * c + 4 * q
                    ins = turn(b[0:m, at:at + 4], row[:, c0:c0 + m])
            end(ins, "cols")
            for n in range(8):
                panel_here(pe, f"v{n // 4}")
                project(("v", n), f"v{n // 4}", 128 * (n % 4), 128)
            pe.wait_ge(tail_done, 16)
            b = begin("convrow")
            end(turn(b[0:96, 0:128], tail[:, :, :, :].rearrange("p a b c -> p (a b c)")), "convrow")
            for n in range(8):
                panel_here(pe, f"o{n // 4}")
                project(("o", n), f"o{n // 4}", 128 * (n % 4), 128)

            for n in range(8):
                taken(pe, "v", n)
            pe.wait_ge(qk_ready, 16)

            def heads_turned(c):
                m = CHUNKS[c][1]
                pe.wait_ge(hn_ready, c + 1)
                b = begin("hT", c)
                for k in range(8):
                    ins = turn(b[:, 64 * k:64 * k + m],
                               num[0:m, c % 2, k // 2, 128 * (k % 2):128 * (k % 2) + 128])
                end(ins, "hT", c)

            for c, (c0, m) in enumerate(CHUNKS):
                q0 = qcol(c0)
                for s in range(2):
                    b = begin("krow", c, s)
                    for k in range(4):
                        ins = turn(b[0:m, 128 * k:128 * k + 128], qk[:, 8 + 4 * s + k, q0:q0 + m])
                    end(ins, "krow", c, s)
                for s in range(2):
                    b = begin("vrow", c, s)
                    for k in range(4):
                        ins = turn(b[0:m, 128 * k:128 * k + 128], vT[:, 4 * s + k, c0:c0 + m])
                    end(ins, "vrow", c, s)
                b = begin("s", c)
                for h in range(4):
                    ins = group(b[0:m, 64 * h:64 * h + m],
                                [(qk[:, 8 + 2 * h + j, q0:q0 + m], qk[:, 2 * h + j, q0:q0 + m]) for j in range(2)])
                end(ins, "s", c)
                pe.wait_ge(q_scaled, c + 1)
                taken(pe, "s", c)
                for s in range(2):
                    taken(pe, "krow", c, s)
                    taken(pe, "vrow", c, s)
                if c == 0:
                    pe.wait_ge(ones_set, 1)
                    pe.wait_ge(ld_mem, 64)
                    pe.wait_ge(n_set, 1)
                else:
                    for n in range(8):
                        taken(pe, "upd", c - 1, n)
                for h in range(4):
                    b = begin("num", c, h)
                    v = vrow[0:m, c % 2, 257 * h:257 * h + 257]
                    pairs = [(sT[0:m, h, 0:m], v)]
                    if c != 1:
                        pairs += [(qk[:, 2 * h + j, q0:q0 + m], C[:, 2 * h + j, :]) for j in range(2)]
                    end(group(b[0:m, 0:257], pairs), "num", c, h)
                for n in range(8):
                    b = begin("upd", c, n)
                    end(group(b[:, 0:257], [(krow[0:m, c % 2, 128 * n:128 * n + 128],
                                             vrow[0:m, c % 2, 257 * (n // 2):257 * (n // 2) + 257])]), "upd", c, n)
                if c in (0, 5):
                    for n in range(8):
                        taken(pe, "upd", c, n)
                    b = begin("nT", c)
                    end(turn(b[0:8, 0:128], C[:, :, 256]), "nT", c)
                if c:
                    heads_turned(c - 1)
            heads_turned(5)

            pe.wait_ge(ld_cache, 32)
            for t in range(4):
                b = begin("cacheT", t)
                turn(b[:, 0:128], cache_row[:, t, 0:128])
                turn(b[:, 128:256], cache_row[:, t, 128:256])
                end(turn(b[0:64, 256:384], cache_row[:, t, 256:320]), "cacheT", t)
            for t in range(4):
                taken(pe, "cacheT", t)
                taken(pe, "kvrow", t)
            panel_here(pe, "ukuv")
            for hp in range(4):
                b = begin("ukT", hp)
                for h in (0, 1):
                    for r in (0, 1):
                        at = 128 * (2 * hp + h)
                        ins = turn(b[:, 256 * h + 128 * r:256 * h + 128 * r + 128], PV["uk"][:, r, at:at + 128])
                end(ins, "ukT", hp)
                w = f"uq{hp // 2}"
                panel_here(pe, w)
                for h in (0, 1):
                    at = 192 * (2 * (hp % 2) + h)
                    project(("qn", hp, h), w, at, 128, cq, 3)
                    project(("qr", hp, h), w, at + 128, 64, cq, 3)
                    taken(pe, "qr", hp, h)
                    b = begin("qrs", hp, h)
                    end(group(b[0:64, 0:NT], [(cst("swap", 64), qx[:, h, :])]), "qrs", hp, h)
                taken(pe, "ukT", hp)
                for h in (0, 1):
                    taken(pe, "qn", hp, h)
                for n in range(4):
                    h, r = n // 2, n % 2
                    b = begin("ql", hp, n)
                    end(group(b[:, 0:NT], [(ukT[:, h, 128 * r:128 * r + 128], qn[:, h, :])]), "ql", hp, n)
                for n in range(4):
                    taken(pe, "ql", hp, n)
                pe.wait_ge(q_ready, 2 * hp + 2)

                def scores(hp, c):
                    c0, m = CHUNKS[c]
                    ql_ = [qlat[:, r, 2 * c0:2 * c0 + 2 * m] for r in (0, 1)]
                    qr_ = qr[:, 2 * c0:2 * c0 + 2 * m]
                    parts = [(cache_lat, 0, PAST, cache_kr), (lat, 0, TS, krT)] if c == 0 else \
                        [(lat, TS, c0 + m - TS, krT)]
                    for p, (kl, k0, n, kr_) in enumerate(parts):
                        b = begin("sc", hp, c, p)
                        end(group(b[0:2 * m, 0:n], [(ql_[r], kl[:, r, k0:k0 + n]) for r in (0, 1)]
                                  + [(qr_, kr_[:, k0:k0 + n])]), "sc", hp, c, p)

                def attend(hp, c, u):
                    c0, m = CHUNKS[c]
                    pr, pt = prob[0:2 * m, u % 2, :], pT[:, u % 2, :, :]
                    pe.wait_ge(pnorm, u + 1)
                    if c == 0:
                        sizes = [(0, k, 128, cache_row[:, k, :]) for k in range(4)] + [(1, 4, TS, kvrow[:, 3, :])]
                    else:
                        n = c0 + m - TS
                        sizes = [(0, k, min(128, n - 128 * k), kvrow[:, k, :]) for k in range((n + 127) // 128)]
                    for p in range(sizes[-1][0] + 1):
                        b = begin("pT", hp, c, p)
                        for pp, k, n, _ in sizes:
                            if pp == p:
                                ins = turn(b[0:n, 128 * (k % 4):128 * (k % 4) + 2 * m], pr[:, 128 * k:128 * k + n])
                        end(ins, "pT", hp, c, p)
                    for p in range(sizes[-1][0] + 1):
                        taken(pe, "pT", hp, c, p)
                    b = begin("ol", hp, c)
                    for r in (0, 1):
                        ins = group(b[:, 128 * r:128 * r + 2 * m],
                                    [(row[0:n, 128 * r:128 * r + 128], pt[0:n, k, 0:2 * m]) for _, k, n, row in sizes])
                    end(ins, "ol", hp, c)

                for c in range(7):
                    if c < 6:
                        scores(hp, c)
                    if c:
                        attend(hp, c - 1, 6 * hp + c - 1)
                for c in range(6):
                    taken(pe, "ol", hp, c)
                for h in (0, 1):
                    b = begin("ov", hp, h)
                    at = 128 * (2 * hp + h)
                    end(group(b[:, 0:NT], [(PV["uv"][:, r, at:at + 128], olat[:, r, h, :]) for r in (0, 1)]),
                        "ov", hp, h)

            for n in range(16):
                panel_here(pe, f"g{n // 4}")
                project(("g", n), f"g{n // 4}", 128 * (n % 4), 128)
            for c in range(6):
                taken(pe, "hT", c)
            for n in range(8):
                panel_here(pe, f"pa{n // 4}")
                project(("ya", n), f"pa{n // 4}", 128 * (n % 4), 128, oT)
            for hp in range(4):
                for h in (0, 1):
                    taken(pe, "ov", hp, h)
            for n in range(8):
                panel_here(pe, f"pb{n // 4}")
                project(("yb", n), f"pb{n // 4}", 128 * (n % 4), 128, ovT)
            pe.wait_ge(mix_a, 8)
            for t, (c0, m) in enumerate(ROWS):
                for s in range(2):
                    panel_here(pe, f"wo{s}")
                    b = begin("out", t, s)
                    end(group(b[0:m, :], [(mixed[:, k, c0:c0 + m], PV[f"wo{s}"][:, k, :]) for k in range(8)]),
                        "out", t, s)
            for t, (c0, m) in enumerate(ROWS):
                pe.wait_ge(x2_ready, t + 1)
                for s in range(2):
                    b = begin("x2T", t, s)
                    for k in range(4):
                        ins = turn(b[:, m * k:m * k + m], x2[0:m, t, 128 * (4 * s + k):128 * (4 * s + k) + 128])
                    end(ins, "x2T", t, s)
            pe.wait_ge(ld_late, 48)
            for t, (c0, m) in enumerate(ROWS):
                for s in range(2):
                    taken(pe, "x2T", t, s)
                b = begin("lg", t)
                end(group(b[0:m, 0:NE], [(x2T[:, k, c0:c0 + m], w_rt[:, k, :]) for k in range(8)]), "lg", t)
            pe.wait_ge(chosen_set, 3)
            for t, (c0, m) in enumerate(ROWS):
                b = begin("pos", t)
                pairs = [(cst("ones")[0:ROWS[s][1], 0:m], chosen[0:ROWS[s][1], s, :]) for s in range(t)]
                pairs += [(cst("below")[0:m, 0:m], chosen[0:m, t, :])]
                end(group(b[0:m, 0:NE], pairs), "pos", t)
            b = begin("cnt")
            end(group(b[:, 0:NE], [(cst("ones")[0:n, :], chosen[0:n, t, :]) for t, (_, n) in enumerate(ROWS)]), "cnt")

            def gather():
                for k in range(8):
                    for t, (_, n) in enumerate(ROWS):
                        ins = pe.matmul(banks[0][:, BLK * k:BLK * k + BLK], x2[0:n, t, 128 * k:128 * k + 128],
                                        pick[0:n, t, :], start=(t == 0), stop=(t == 2))
                ins.then_inc(m_gath, 1)

            pe.wait_ge(moe_tab, 1)
            taken(pe, "cnt")
            for t in range(3):
                taken(pe, "pos", t)
            nb = pe.value_load(nbi[0:1, 0:1].bitcast(I32), min_val=NE, max_val=MAXB)
            pe.wait_ge(m_pick, 1)
            gather()
            with pe.Fori(0, nb) as b:
                pe.wait_ge(m_xg, b + 1)
                for c in range(4):
                    pe.wait_ge(chunk_in[c], 16 * b + 16)
                    w = up_w(c)
                    for k in range(2):
                        for n in range(16):
                            ins = pe.matmul(banks[1 + n // 8][:, BLK * (n % 8):BLK * (n % 8) + BLK],
                                            w[:, k, 128 * n:128 * n + 128], xg[:, 2 * c + k, :],
                                            start=(c == 0 and k == 0 and n % 8 == 0), stop=(c == 3 and k == 1),
                                            skip_group_check=True)
                    ins.then_inc(m_used, 1)
                pe.wait_ge(m_pick, b + 2)
                gather()
                pe.wait_ge(m_hid, b + 1)
                for c in range(2):
                    pe.wait_ge(chunk_in[4 + c], 16 * b + 16)
                    w = dn_w(c)
                    for k in range(4):
                        for n in range(8):
                            ins = pe.matmul(banks[3][:, BLK * n:BLK * n + BLK], w[:, k, 128 * n:128 * n + 128],
                                            hid[:, 4 * c + k, :], start=(c == 0 and k == 0 and n == 0),
                                            stop=(c == 1 and k == 3), skip_group_check=True)
                    ins.then_inc(m_used, 1)
                pe.wait_ge(m_yt, b + 1)
                pe.matmul(banks[4][0:BLK, 0:128], yT[:, 0, :], ident, start=True, stop=True)
                for n in range(1, 8):
                    ins = turn(banks[4 + n // 4][0:BLK, 128 * (n % 4):128 * (n % 4) + 128], yT[:, n, :])
                ins.then_inc(m_tr, 1)

        @block.scalar
        def _(act):
            steps = [0]

            def step(ins):
                steps[0] += 1
                ins.then_inc(act_step, 1)
                act.wait_ge(act_step, steps[0])

            def take(ins, *name):
                n = JOB[name]
                ins.then_inc(bank_free[n % 8], 1)
                act.wait_ge(bank_free[n % 8], n // 8 + 1)

            def signal(ins, s, v):
                ins.then_inc(s, 1)
                act.wait_ge(s, v)

            def copy(out, src, scale=1.0):
                return act.activation(out, src, ACT.Copy, scale=scale)

            act.wait_ge(ld_x, 80)
            for t, (_, n) in enumerate(ROWS):
                signal(act.activation(xn_rows[0:n, t, :], x_rows[0:n, t, :], ACT.Square, accum_out=ss[0:n, t:t + 1]),
                       rms_s, t + 1)
            for t, (_, n) in enumerate(ROWS):
                act.wait_ge(rms_v, t + 1)
                signal(act.activation(ss[0:n, t:t + 1], ss[0:n, t:t + 1], ACT.Sqrt), rms_s, 4 + t)
            filled(act, "vecT")
            take(copy(vec[:, 0:NVEC], bank(("vecT",))[:, 0:NVEC]), "vecT")
            filled(act, "convT")
            take(copy(convst[:, :, :], bank(("convT",))[:, 0:48].rearrange("p (j c) -> p j c", j=3)), "convT")
            filled(act, "buT")
            take(copy(bu_t[:, :, :], bank(("buT",))[:, :].rearrange("p (c e) -> p c e", c=16)), "buT")
            filled(act, "bdT")
            take(copy(bd_t[:, :, :], bank(("bdT",))[:, 0:256].rearrange("p (c e) -> p c e", c=8)), "bdT")
            for n in range(3):
                filled(act, "cq", n)
                signal(act.activation(sq[:, n, :], bank(("cq", n))[:, 0:NT], ACT.Square), cq_ready, n + 1)
                take(copy(cq[:, n, :], bank(("cq", n))[:, 0:NT], vec[:, V_GQ + n:V_GQ + n + 1]), "cq", n)
            for n in range(2):
                filled(act, "ckv", n)
                signal(act.activation(sq[:, 3 + n, :], bank(("ckv", n))[:, 0:NT], ACT.Square), cq_ready, n + 4)
                take(copy(lat[:, n, :], bank(("ckv", n))[:, 0:NT]), "ckv", n)
            filled(act, "kr")
            take(copy(kr_raw, bank(("kr",))[0:64, 0:NT]), "kr")
            for n, r in enumerate((rq, rk)):
                act.wait_ge(low_v, n + 1)
                signal(act.activation(r, r, ACT.Sqrt), low_s, n + 1)
            act.wait_ge(lg_d, 1)
            signal(act.activation(R_MX, R_A, ACT.Exp), lg_a, 1)
            act.wait_ge(lg_d, 2)
            signal(act.activation(R_MX, R_MX, ACT.Ln), lg_a, 2)
            act.wait_ge(gates_x, 1)
            step(act.activation(R_WI, R_WI, ACT.Exp, scale=-1.0))
            step(act.activation(R_DN, R_DN, ACT.Exp, scale=-1.0))
            signal(act.activation(R_WK, R_WK, ACT.Exp), gates4, 1)

            def sigmoid_qk(n):
                act.wait_ge(conv_done, n + 1)
                if n >= 2:
                    act.wait_ge(qk_ready, n - 1)
                signal(act.activation(sig[:, n % 2, :], qk[:, n, :], ACT.Sigmoid), sig_ready, n + 1)

            act.wait_ge(pad_set, 1)
            for n in range(16):
                if n == 8:
                    for t, (c0, m) in enumerate(KEYS):
                        filled(act, "kvrow", t)
                        take(copy(kvrow[0:m, t, :], bank(("kvrow", t))[0:m, 0:320]), "kvrow", t)
                filled(act, "qk", n)
                if n >= 2:
                    act.wait_ge(conv_done, n - 1)
                    act.wait_ge(tail_done, n - 1)
                p = bank(("qk", n))
                step(copy(u_pad[:, n % 2, 0:3], convst[:, :, n]))
                step(copy(u_pad[:, n % 2, 3:67], p[:, 0:64]))
                take(copy(u_pad[:, n % 2, 70:342], p[:, 64:NT]), "qk", n)
                if n:
                    sigmoid_qk(n - 1)
            sigmoid_qk(15)
            for h in range(4):
                filled(act, "wi", h)
                take(copy(wib[:, h, :], bank(("wi", h))[:, 0:NT]), "wi", h)
                step(copy(wprev[:, h, 0:1], wib[:, h, 63:64]))
                signal(copy(wprev[:, h, 1:6], wib[:, h, 79:NT:64]), wprev_ready, h + 1)
            for n in range(8):
                filled(act, "v", n)
                take(copy(vT[:, n, :], bank(("v", n))[:, 0:NT]), "v", n)
            filled(act, "convrow")
            take(copy(tailrow[:, :], bank(("convrow",))[0:96, 0:128]), "convrow")
            for n in range(8):
                filled(act, "o", n)
                take(act.activation(oT[:, n, :], bank(("o", n))[:, 0:NT], ACT.Sigmoid), "o", n)

            for h in range(4):
                taken(act, "mx", h)
            taken(act, "cols")
            for c, (c0, m) in enumerate(CHUNKS):
                if c:
                    taken(act, "s", c - 1)
                for h in range(4):
                    signal(act.activation(wexp[0:m, h, 0:m], emat[0:m, h, c0:c0 + m], ACT.Exp,
                                          bias=colT[0:m, c, 0, h:h + 1]), e_ready, 4 * c + h + 1)
                if c >= 2:
                    filled(act, "upd", c - 2, 7)
                for s in range(2):
                    filled(act, "krow", c, s)
                    p = bank(("krow", c, s))
                    h = 2 * s
                    step(copy(krow[0:m, c % 2, 256 * h:256 * h + 256], p[0:m, 0:256], colT[0:m, c, 2, h:h + 1]))
                    take(copy(krow[0:m, c % 2, 256 * h + 256:256 * h + 512], p[0:m, 256:512],
                              colT[0:m, c, 2, h + 1:h + 2]), "krow", c, s)
                for s in range(2):
                    filled(act, "vrow", c, s)
                    v = vrow[0:m, c % 2, :].rearrange("p (h e) -> p h e", h=4)[:, 2 * s:2 * s + 2, 0:256]
                    take(copy(v, bank(("vrow", c, s))[0:m, :].rearrange("p (h e) -> p h e", h=2)), "vrow", c, s)
                if c >= 2:
                    filled(act, "hT", c - 2)
                elif c == 1:
                    act.wait_ge(rows_zeroed, 16)
                for h in range(4):
                    filled(act, "num", c, h)
                    p = bank(("num", c, h))
                    if c or h:
                        pass
                    step(act.activation(junk[0:m, 0:256], p[0:m, 0:256], ACT.Square, accum_out=hs[0:m, 0, h:h + 1]))
                    take(copy(num[0:m, c % 2, h, :], p[0:m, 0:257]), "num", c, h)
                act.wait_ge(hs_v, c + 1)
                signal(act.activation(hs[0:m, 4, :], hs[0:m, 3, :], ACT.Sqrt), hs_s, c + 1)
                if c in (0, 5):
                    filled(act, "nT", c)
                    take(copy(nrow[:, c // 5, :], bank(("nT", c))[0:8, 0:128]), "nT", c)

            for t in range(4):
                filled(act, "cacheT", t)
                p = bank(("cacheT", t))
                step(copy(cache_lat[:, :, 128 * t:128 * t + 128], p[:, 0:256].rearrange("p (r t) -> p r t", r=2)))
                take(copy(cache_kr[:, 128 * t:128 * t + 128], p[0:64, 256:384]), "cacheT", t)
            for hp in range(4):
                filled(act, "ukT", hp)
                take(copy(ukT[:, :, :], bank(("ukT", hp))[:, :].rearrange("p (h r) -> p h r", h=2)), "ukT", hp)
                for n in range(4):
                    filled(act, "ql", hp, n)
                    for j, (dst, src) in enumerate(by_chunk(qlat[:, n % 2, :], n // 2, bank(("ql", hp, n))[:, 0:NT])):
                        if j < 2:
                            step(copy(dst, src))
                        else:
                            take(copy(dst, src), "ql", hp, n)
                for c in range(7):
                    if c < 6:
                        u, m = 6 * hp + c, CHUNKS[c][1]
                        act.wait_ge(pmax, u + 1)
                        if u >= 2:
                            filled(act, "pT", (u - 2) // 6, (u - 2) % 6, 1 if (u - 2) % 6 == 0 else 0)
                        parts = [(0, PAST), (PAST, TS)] if c == 0 else [(0, CHUNKS[c][0] + m - TS)]
                        for p, (at, n) in enumerate(parts):
                            take(act.activation(prob[0:2 * m, u % 2, at:at + n], bank(("sc", hp, c, p))[0:2 * m, 0:n],
                                                ACT.Exp, bias=st[0:2 * m, u % 2, 3:4], scale=SCALE,
                                                accum_out=st[0:2 * m, u % 2, 4 + p:5 + p]), "sc", hp, c, p)
                    if c:
                        u, (c0, m) = 6 * hp + c - 1, CHUNKS[c - 1]
                        n = c0 + m - TS
                        if u >= 2:
                            filled(act, "ol", (u - 2) // 6, (u - 2) % 6)
                        filled(act, "pT", hp, c - 1, 0)
                        p = bank(("pT", hp, c - 1, 0))[:, :].rearrange("p (k q) -> p k q", k=4)
                        if c == 1:
                            take(copy(pT[:, u % 2, 0:4, :], p), "pT", hp, 0, 0)
                            filled(act, "pT", hp, 0, 1)
                            take(copy(pT[0:64, u % 2, 4, :], bank(("pT", hp, 0, 1))[0:64, 0:128]), "pT", hp, 0, 1)
                        else:
                            f, rest = n // 128, n % 128
                            if f:
                                step(copy(pT[:, u % 2, 0:f, 0:2 * m], p[:, 0:f, 0:2 * m]))
                            take(copy(pT[0:rest, u % 2, f, 0:2 * m], p[0:rest, f, 0:2 * m]), "pT", hp, c - 1, 0)
                for h in (0, 1):
                    filled(act, "ov", hp, h)
                    take(copy(ovT[:, 2 * hp + h, :], bank(("ov", hp, h))[:, 0:NT]), "ov", hp, h)
            for n in range(16):
                filled(act, "g", n)
                take(act.activation(gates[:, n, :], bank(("g", n))[:, 0:NT], ACT.Sigmoid), "g", n)

            for t, (_, n) in enumerate(ROWS):
                taken(act, "out", t, 0)
                taken(act, "out", t, 1)
                signal(act.activation(x2[0:n, t, :], x1[0:n, t, :], ACT.Square, accum_out=ss[0:n, 8 + t:9 + t]),
                       x1_ss, t + 1)
                act.wait_ge(x1_v, t + 1)
                signal(act.activation(ss[0:n, 8 + t:9 + t], ss[0:n, 8 + t:9 + t], ACT.Sqrt), x1_s, t + 1)
            for t, (c0, m) in enumerate(ROWS):
                for s in range(2):
                    filled(act, "x2T", t, s)
                    take(copy(x2T[:, 4 * s:4 * s + 4, c0:c0 + m],
                              bank(("x2T", t, s))[:, 0:4 * m].rearrange("p (k t) -> p k t", k=4)), "x2T", t, s)
            for t, (_, n) in enumerate(ROWS):
                act.wait_ge(gate_x, t + 1)
                signal(act.activation(gate[0:n, t, 0:4], gate[0:n, t, 0:4], ACT.Exp, accum_out=gsum[0:n, t:t + 1]),
                       gate_e, t + 1)

            act.wait_ge(moe_tab, 1)
            nb = act.value_load(nbi[0:1, 0:1].bitcast(I32), min_val=NE, max_val=MAXB)
            act.wait_ge(m_gath, 1)
            signal(copy(xg, banks[0][:, :].rearrange("p (k s) -> p k s", k=8)), m_xg, 1)
            with act.Fori(0, nb) as b:
                act.wait_ge(m_gt, b + 1)
                act.activation(sg, gt, ACT.Sigmoid, scale=ALPHA).then_inc(m_sig, 1)
                act.wait_ge(m_gath, b + 2)
                act.wait_ge(m_sig, b + 1)
                copy(xg, banks[0][:, :].rearrange("p (k s) -> p k s", k=8)).then_inc(m_xg, 1)
                act.wait_ge(m_tr, b + 1)
                act.wait_ge(yrow_free, b + 1)
                act.wait_ge(m_xg, b + 2)
                copy(yrow[:, 0:512], banks[4][0:BLK, :]).then_inc(m_act, 1)
                act.wait_ge(m_act, b + 1)
                copy(yrow[:, 512:1024], banks[5][0:BLK, :]).then_inc(m_yrow, 1)
                act.wait_ge(m_yrow, b + 1)
                act.wait_ge(moe_tab, 1)
                act.nop()

            for t, (_, n) in enumerate(ROWS):
                act.wait_ge(fin_v, 2 * t + 1)
                signal(act.activation(x2[0:n, t, :], x1[0:n, t, :], ACT.Square, accum_out=ss[0:n, 12 + t:13 + t]),
                       fin_ss, t + 1)
                act.wait_ge(fin_v, 2 * t + 2)
                signal(act.activation(ss[0:n, 12 + t:13 + t], ss[0:n, 12 + t:13 + t], ACT.Sqrt), fin_s, t + 1)

        @block.vector
        def _(dve):
            steps = [0]

            def step(ins):
                steps[0] += 1
                ins.then_inc(dve_step, 1)
                dve.wait_ge(dve_step, steps[0])

            def take(ins, *name):
                n = JOB[name]
                ins.then_inc(bank_free[n % 8], 1)
                dve.wait_ge(bank_free[n % 8], n // 8 + 1)

            def signal(ins, s, v):
                ins.then_inc(s, 1)
                dve.wait_ge(s, v)

            def ts(out, a, s1, op0, s2=None, op1=ALU.bypass):
                return dve.tensor_scalar(out, a, s1, s2, op0, op1)

            def tt(out, a, b, op):
                return dve.tensor_tensor(out, a, b, op)

            def stt(out, a, s, b, op0, op1):
                return dve.scalar_tensor_tensor(out=out, in0=a, scalar=s, in1=b, op0=op0, op1=op1)

            dve.wait_ge(ld_x, 80)
            for t, (_, n) in enumerate(ROWS):
                dve.wait_ge(rms_s, 3)
                signal(ts(ss[0:n, t:t + 1], ss[0:n, t:t + 1], 1.0 / D, ALU.mult, EPS, ALU.add), rms_v, t + 1)
            for t, (_, n) in enumerate(ROWS):
                dve.wait_ge(rms_s, 4 + t)
                step(dve.reciprocal(ss[0:n, t:t + 1], ss[0:n, t:t + 1]))
                signal(ts(xn_rows[0:n, t, :], x_rows[0:n, t, :], ss[0:n, t:t + 1], ALU.mult), xn_ready, t + 1)
            taken(dve, "vecT")
            for t, (c0, m) in enumerate(ROWS):
                for s in range(2):
                    filled(dve, "xT", t, s)
                    g = vec[:, V_GMIX + 4 * s:V_GMIX + 4 * s + 4].unsqueeze(2).broadcast_to([128, 4, m])
                    take(tt(xT[:, 4 * s:4 * s + 4, c0:c0 + m],
                            bank(("xT", t, s))[:, 0:4 * m].rearrange("p (k t) -> p k t", k=4), g, ALU.mult),
                         "xT", t, s)
            dve.wait_ge(ld_mem, 64)
            step(dve.memset(mst[:, 1:2], 0.0))
            signal(dve.tensor_copy(C[:, :, 256], vec[:, V_N0:V_N0 + 8]), n_set, 1)
            filled(dve, "ig")
            take(ts(R_IG, bank(("ig",))[0:4, 0:NT], b_if[:, 0:1], ALU.add), "ig")
            filled(dve, "fg")
            take(ts(R_LF, bank(("fg",))[0:4, 0:NT], b_if[:, 1:2], ALU.add), "fg")
            for n, (name, r, w) in enumerate((("ssq", rq, QL), ("ssk", rk, KVL))):
                filled(dve, name)
                ins = ts(r, bank((name,))[:, 0:NT], 1.0 / w, ALU.mult, EPS, ALU.add)
                take(ins, name)
                signal(dve.engine_nop() if False else ts(ss[:, 15:16], r[:, 0:1], 1.0, ALU.mult), low_v, n + 1)
            filled(dve, "krs")
            take(tt(kr_tmp, bank(("krs",))[0:64, 0:NT], cst("sin", 64), ALU.mult), "krs")
            step(tt(krT, kr_raw, cst("cos", 64), ALU.mult))
            signal(tt(krT, krT, kr_tmp, ALU.add), kr_ready, 1)
            for n, r in enumerate((rq, rk)):
                dve.wait_ge(low_s, n + 1)
                step(dve.reciprocal(r, r))
            for n in range(2):
                signal(stt(lat[:, n, :], lat[:, n, :], vec[:, V_GKV + n:V_GKV + n + 1], rk, ALU.mult, ALU.mult),
                       kv_ready, n + 1)
            step(ts(R_B, R_LF, 0.0, ALU.min))
            step(ts(R_A, R_LF, 0.0, ALU.max))
            signal(tt(R_A, R_B, R_A, ALU.subtract), lg_d, 1)
            dve.wait_ge(lg_a, 1)
            signal(ts(R_MX, R_MX, 1.0, ALU.add), lg_d, 2)
            dve.wait_ge(lg_a, 2)
            step(tt(R_LF, R_B, R_MX, ALU.subtract))
            for c0, m in CHUNKS:
                s = slice(c0, c0 + m)
                step(dve.tensor_tensor_scan(R_B[:, s], cst("ones", 4)[:, 0:m], R_LF[:, s], 0.0, ALU.mult, ALU.add))
            step(tt(R_A, R_IG, R_B, ALU.subtract))
            for c, (c0, m) in enumerate(CHUNKS):
                s, e = slice(c0, c0 + m), slice(c0 + m - 1, c0 + m)
                step(dve.tensor_tensor_scan(R_MX[:, s], R_A[:, s], R_A[:, s], mst[:, c:c + 1], ALU.max, ALU.max))
                new = 8 if c == 0 else c + 1
                step(tt(mst[:, new:new + 1], R_B[:, e], R_MX[:, e], ALU.add))
                step(ts(R_WI[:, s], R_MX[:, s], mst[:, c:c + 1], ALU.subtract))
                step(ts(R_WK[:, s], R_A[:, s], R_MX[:, e], ALU.subtract))
            signal(tt(R_DN, R_B, R_MX, ALU.add), gates_x, 1)

            def silu(n):
                dve.wait_ge(sig_ready, n + 1)
                signal(stt(qk[:, n, :], qk[:, n, :], 1.0 if n < 8 else 1.0 / 16, sig[:, n % 2, :],
                           ALU.mult, ALU.mult), qk_ready, n + 1)

            for n in range(16):
                taken(dve, "qk", n)
                u = u_pad[:, n % 2, :]

                def w(j):
                    return vec[:, V_WCONV + 16 * j + n:V_WCONV + 16 * j + n + 1]

                step(ts(qk[:, n, :], u[:, 0:339], w(0), ALU.mult, vec[:, V_BCONV + n:V_BCONV + n + 1], ALU.add))
                for j in (1, 2):
                    step(stt(qk[:, n, :], u[:, j:j + 339], w(j), qk[:, n, :], ALU.mult, ALU.add))
                signal(stt(qk[:, n, :], u[:, 3:342], w(3), qk[:, n, :], ALU.mult, ALU.add), conv_done, n + 1)
                if n:
                    silu(n - 1)
            silu(15)
            for h in range(4):
                filled(dve, "mx", h)
                take(stt(emat[:, h, :], bank(("mx", h))[0:64, 0:NT], -1.0, cst("mask", 64), ALU.mult, ALU.add),
                     "mx", h)
            filled(dve, "cols")
            p = bank(("cols",))
            step(dve.tensor_copy(colT[:, 0, :, :], p[0:64, 0:12].rearrange("p (a b) -> p a b", a=3)))
            step(dve.tensor_copy(colT[0:16, 1, :, :], p[0:16, 12:24].rearrange("p (a b) -> p a b", a=3)))
            take(dve.tensor_copy(colT[:, 2:6, :, :], p[0:64, 24:72].rearrange("p (c a b) -> p c a b", c=4, a=3)),
                 "cols")
            for n in range(8):
                taken(dve, "o", n)
                step(ts(oT[:, n, :], oT[:, n, :], vec[:, V_GMH + n:V_GMH + n + 1], ALU.mult))

            def heads_out(c):
                c0, m = CHUNKS[c]
                filled(dve, "hT", c)
                take(tt(oT[:, :, c0:c0 + m],
                        bank(("hT", c))[:, :].rearrange("p (k t) -> p k t", k=8)[:, :, 0:m],
                        oT[:, :, c0:c0 + m], ALU.mult), "hT", c)

            dve.wait_ge(wprev_ready, 4)
            for c, (c0, m) in enumerate(CHUNKS):
                q0 = qcol(c0)
                if c:
                    filled(dve, "num", c - 1, 3)
                dve.wait_ge(e_ready, 4 * c + 4)
                filled(dve, "s", c)
                take(tt(sT[0:m, :, 0:m], bank(("s", c))[0:m, 0:256].rearrange("p (h l) -> p h l", h=4)[:, :, 0:m],
                        wexp[0:m, :, 0:m], ALU.mult), "s", c)
                for h in range(4):
                    q = qk[:, 2 * h:2 * h + 2, q0:q0 + m]
                    ins = tt(q, q, wib[:, h:h + 1, c0:c0 + m].broadcast_to([128, 2, m]), ALU.mult)
                    if h < 3:
                        step(ins)
                    else:
                        signal(ins, q_scaled, c + 1)
                for h in range(4):
                    taken(dve, "num", c, h)
                qn_ = num[0:m, c % 2, :, 256]
                step(stt(hs[0:m, 1, :], qn_, -1.0, qn_, ALU.mult, ALU.max))
                step(tt(hs[0:m, 1, :], hs[0:m, 1, :], colT[0:m, c, 1, :], ALU.max))
                step(dve.reciprocal(hs[0:m, 2, :], hs[0:m, 1, :]))
                step(tt(hs[0:m, 3, :], hs[0:m, 2, :], hs[0:m, 2, :], ALU.mult))
                step(tt(hs[0:m, 3, :], hs[0:m, 3, :], hs[0:m, 0, :], ALU.mult))
                signal(ts(hs[0:m, 3, :], hs[0:m, 3, :], 1.0 / 256, ALU.mult, EPS, ALU.add), hs_v, c + 1)
                if c == 1:
                    dve.wait_ge(stored_c, 16)
                    filled(dve, "nT", 0)
                for n in range(8):
                    filled(dve, "upd", c, n)
                    p = bank(("upd", c, n))[:, 0:257]
                    if c == 1:
                        take(dve.tensor_copy(C[:, n, :], p), "upd", c, n)
                    else:
                        take(stt(C[:, n, :], C[:, n, :], wprev[:, n // 2, c:c + 1], p, ALU.mult, ALU.add),
                             "upd", c, n)
                dve.wait_ge(hs_s, c + 1)
                step(dve.reciprocal(hs[0:m, 5, :], hs[0:m, 4, :]))
                step(tt(hs[0:m, 5, :], hs[0:m, 5, :], hs[0:m, 2, :], ALU.mult))
                for h in range(4):
                    ins = ts(num[0:m, c % 2, h, 0:256], num[0:m, c % 2, h, 0:256], hs[0:m, 5, h:h + 1], ALU.mult)
                    if h < 3:
                        step(ins)
                    else:
                        signal(ins, hn_ready, c + 1)
                if c:
                    heads_out(c - 1)
            heads_out(5)

            for hp in range(4):
                for h in (0, 1):
                    filled(dve, "qn", hp, h)
                    take(tt(qn[:, h, :], bank(("qn", hp, h))[:, 0:NT], rq, ALU.mult), "qn", hp, h)
                    filled(dve, "qr", hp, h)
                    take(tt(qx[:, h, :], bank(("qr", hp, h))[0:64, 0:NT], rq[0:64, :], ALU.mult), "qr", hp, h)
                    filled(dve, "qrs", hp, h)
                    take(tt(qtmp, bank(("qrs", hp, h))[0:64, 0:NT], cst("sin", 64), ALU.mult), "qrs", hp, h)
                    step(tt(qx[:, h, :], qx[:, h, :], cst("cos", 64), ALU.mult))
                    for j, ((dst, a), (_, b)) in enumerate(zip(by_chunk(qr, h, qx[:, h, :]), by_chunk(qr, h, qtmp))):
                        ins = tt(dst, a, b, ALU.add)
                        if j < 2:
                            step(ins)
                        else:
                            signal(ins, q_ready, 2 * hp + h + 1)
                for c in range(7):
                    if c < 6:
                        u, m = 6 * hp + c, CHUNKS[c][1]
                        s = st[0:2 * m, u % 2, :]
                        parts = [PAST, TS] if c == 0 else [CHUNKS[c][0] + m - TS]
                        for p, n in enumerate(parts):
                            filled(dve, "sc", hp, c, p)
                            step(dve.tensor_reduce(s[:, p:p + 1], bank(("sc", hp, c, p))[0:2 * m, 0:n], AX.X, ALU.max))
                        if c == 0:
                            step(tt(s[:, 0:1], s[:, 0:1], s[:, 1:2], ALU.max))
                        signal(ts(s[:, 3:4], s[:, 0:1], -SCALE, ALU.mult), pmax, u + 1)
                    if c:
                        u, (c0, m) = 6 * hp + c - 1, CHUNKS[c - 1]
                        n = PAST + TS if c == 1 else c0 + m - TS
                        s = st[0:2 * m, u % 2, :]
                        for p in range(2 if c == 1 else 1):
                            taken(dve, "sc", hp, c - 1, p)
                        if c == 1:
                            step(tt(s[:, 4:5], s[:, 4:5], s[:, 5:6], ALU.add))
                        step(dve.reciprocal(s[:, 6:7], s[:, 4:5]))
                        signal(ts(prob[0:2 * m, u % 2, 0:n], prob[0:2 * m, u % 2, 0:n], s[:, 6:7], ALU.mult),
                               pnorm, u + 1)
                        filled(dve, "ol", hp, c - 1)
                        p = bank(("ol", hp, c - 1))[:, 0:256].rearrange("p (r q) -> p r q", r=2)[:, :, 0:2 * m]
                        for r in (0, 1):
                            ins = dve.tensor_copy(olat[:, r, :, c0:c0 + m],
                                                  p[:, r, :].rearrange("p (h t) -> p h t", h=2))
                            if r:
                                take(ins, "ol", hp, c - 1)
                            else:
                                step(ins)
            for n in range(8):
                taken(dve, "g", n)
                filled(dve, "ya", n)
                take(tt(mixed[:, n, :], bank(("ya", n))[:, 0:NT], gates[:, n, :], ALU.mult), "ya", n)
            for n in range(8):
                taken(dve, "g", 8 + n)
                filled(dve, "yb", n)
                take(tt(sig[:, 0, 0:NT], bank(("yb", n))[:, 0:NT], gates[:, 8 + n, :], ALU.mult), "yb", n)
                signal(tt(mixed[:, n, :], mixed[:, n, :], sig[:, 0, 0:NT], ALU.add), mix_a, n + 1)
            dve.wait_ge(ld_x1, 80)
            for t, (_, m) in enumerate(ROWS):
                for s in range(2):
                    filled(dve, "out", t, s)
                    x = x1[0:m, t, 512 * s:512 * s + 512]
                    take(tt(x, bank(("out", t, s))[0:m, :], x, ALU.add), "out", t, s)
            dve.wait_ge(ld_late, 48)
            for t, (_, m) in enumerate(ROWS):
                r = ss[0:m, 8 + t:9 + t]
                dve.wait_ge(x1_ss, t + 1)
                signal(ts(r, r, 1.0 / D, ALU.mult, EPS, ALU.add), x1_v, t + 1)
                dve.wait_ge(x1_s, t + 1)
                step(dve.reciprocal(r, r))
                signal(stt(x2[0:m, t, :], x1[0:m, t, :], r, g_ffn_b[0:m, :], ALU.mult, ALU.mult), x2_ready, t + 1)

            for t, (_, m) in enumerate(ROWS):
                filled(dve, "lg", t)
                take(tt(logit[0:m, t, :], bank(("lg", t))[0:m, 0:NE], b_router_b[0:m, :], ALU.add), "lg", t)
                step(dve.max(top[0:m, t, :], logit[0:m, t, :]))
                step(dve.max_index(topi[0:m, t, :].bitcast(U32), top[0:m, t, :], logit[0:m, t, :]))
                step(dve.tensor_copy(topif[0:m, t, :], topi[0:m, t, :].bitcast(U32)))
                for k in range(4):
                    step(ts(onehot[0:m, t, k, :], cst("expert")[0:m, :], topif[0:m, t, k:k + 1], ALU.is_equal))
                c = chosen[0:m, t, :]
                step(tt(c, onehot[0:m, t, 0, :], onehot[0:m, t, 1, :], ALU.add))
                step(tt(c, c, onehot[0:m, t, 2, :], ALU.add))
                signal(tt(c, c, onehot[0:m, t, 3, :], ALU.add), chosen_set, t + 1)
                signal(ts(gate[0:m, t, 0:4], top[0:m, t, 0:4], top[0:m, t, 0:1], ALU.subtract), gate_x, t + 1)
            for t, (_, m) in enumerate(ROWS):
                dve.wait_ge(gate_e, t + 1)
                step(dve.reciprocal(gsum[0:m, t:t + 1], gsum[0:m, t:t + 1]))
                step(ts(gate[0:m, t, 0:4], gate[0:m, t, 0:4], gsum[0:m, t:t + 1], ALU.mult))
            for t, (_, m) in enumerate(ROWS):
                filled(dve, "pos", t)
                take(dve.tensor_copy(posm[0:m, t, :], bank(("pos", t))[0:m, 0:NE]), "pos", t)
            filled(dve, "cnt")
            cnt = bank(("cnt",))[:, 0:NE]
            step(ts(nblk, cnt, float(BLK), ALU.is_gt, 1.0, ALU.add))
            more = range(2 * BLK, NT, BLK)
            for n in more:
                ins = stt(nblk, cnt, float(n), nblk, ALU.is_gt, ALU.add)
                if n == more[-1]:
                    take(ins, "cnt")
                else:
                    step(ins)
            step(dve.tensor_tensor_scan(pend, cst("ones")[:, 0:NE], nblk, 0.0, ALU.mult, ALU.add))
            step(tt(start, pend, nblk, ALU.subtract))
            cmp = r_o[0:1, 0:NB1 * NE].rearrange("p (b e) -> p b e", e=NE)
            step(tt(cmp, cst("block", 1).unsqueeze(2).broadcast_to([1, NB1, NE]),
                    pend[0:1, :].unsqueeze(1).broadcast_to([1, NB1, NE]), ALU.is_ge))
            step(dve.tensor_reduce(be[0:1, :], cmp, AX.X, ALU.add))
            step(ts(be[0:1, :], be[0:1, :], float(NE - 1), ALU.min))
            step(dve.tensor_copy(bei[0:1, :].bitcast(I32), be[0:1, :]))
            signal(dve.tensor_copy(nbi[0:1, 0:1].bitcast(I32), pend[0:1, NE - 1:NE]), moe_tab, 1)
            for t, (_, m) in enumerate(ROWS):
                step(stt(posm[0:m, t, :], start[0:m, :], float(BLK), posm[0:m, t, :], ALU.mult, ALU.add))
                for k in range(4):
                    d = dest[0:m, t, k:k + 1]
                    step(dve.tensor_tensor_reduce(t32[0:m, :], onehot[0:m, t, k, :], posm[0:m, t, :], 1.0, 0.0,
                                                  ALU.mult, ALU.add, d))
                    step(ts(t1[0:m, :], cst("block")[0:m, :], -float(BLK), ALU.mult, d, ALU.add))
                    step(ts(t2[0:m, :], t1[0:m, :], -1.0, ALU.max, 1.0, ALU.add))
                    if k == 0:
                        step(stt(loc[0:m, t, :], t1[0:m, :], float(BLK), t2[0:m, :], ALU.is_lt, ALU.mult))
                    else:
                        step(stt(t2[0:m, :], t1[0:m, :], float(BLK), t2[0:m, :], ALU.is_lt, ALU.mult))
                        step(tt(loc[0:m, t, :], loc[0:m, t, :], t2[0:m, :], ALU.add))
                step(ts(loc[0:m, t, :], loc[0:m, t, :], -1.0, ALU.add))
                signal(dve.tensor_copy(desti[0:m, t, :].bitcast(U32), dest[0:m, t, :]), desti_set, t + 1)

            for t, (_, m) in enumerate(ROWS):
                ins = ts(pick[0:m, t, :], cst("slot")[0:m, :], loc[0:m, t, 0:1], ALU.is_equal)
                if t < 2:
                    step(ins)
                else:
                    signal(ins, m_pick, 1)
            nb = dve.value_load(nbi[0:1, 0:1].bitcast(I32), min_val=NE, max_val=MAXB)
            dve.wait_ge(moe_tab, 1)
            with dve.Fori(0, nb) as b:
                e = dve.value_load(bei[0:1, bass.ds(b, 1)].bitcast(I32), min_val=0, max_val=NE - 1)
                bias_g = bu_t[:, 0:8, bass.ds(e, 1)].broadcast_to([128, 8, BLK])
                bias_u = bu_t[:, 8:16, bass.ds(e, 1)].broadcast_to([128, 8, BLK])
                bias_d = bd_t[:, :, bass.ds(e, 1)].broadcast_to([128, 8, BLK])

                def order(ins, n):
                    ins.then_inc(m_dve, 1)
                    dve.wait_ge(m_dve, 6 * b + n)

                def blk(n):
                    return banks[n][:, :].rearrange("p (k s) -> p k s", k=8)

                dve.wait_ge(m_gath, b + 1)
                for t, (_, m) in enumerate(ROWS):
                    ins = ts(pick[0:m, t, :], cst("slot")[0:m, :], loc[0:m, t, bass.ds(b + 1, 1)], ALU.is_equal)
                    if t < 2:
                        order(ins, t + 1)
                    else:
                        ins.then_inc(m_pick, 1)
                        dve.wait_ge(m_pick, b + 2)
                dve.wait_ge(m_used, 6 * b + 4)
                order(tt(gt, blk(1), bias_g, ALU.add), 3)
                ts(gt, gt, LIMIT, ALU.min).then_inc(m_gt, 1)
                dve.wait_ge(m_gt, b + 1)
                order(tt(up, blk(2), bias_u, ALU.add), 4)
                order(ts(up, up, LIMIT, ALU.min, -LIMIT, ALU.max), 5)
                order(stt(up, up, 1.0, gt, ALU.add, ALU.mult), 6)
                dve.wait_ge(m_sig, b + 1)
                tt(hid, up, sg, ALU.mult).then_inc(m_hid, 1)
                dve.wait_ge(m_used, 6 * b + 6)
                tt(yT, blk(3), bias_d, ALU.add).then_inc(m_yt, 1)
                dve.wait_ge(m_yt, b + 1)
                dve.wait_ge(moe_tab, 1)
                dve.nop()

            for t, (_, m) in enumerate(ROWS):
                dve.wait_ge(fin_y[t], 64)
                for k in range(4):
                    y = ring[0:m, (4 * t + k) * D:(4 * t + k + 1) * D]
                    ins = stt(x1[0:m, t, :], y, gate[0:m, t, k:k + 1], x1[0:m, t, :], ALU.mult, ALU.add)
                    if k < 3:
                        step(ins)
                    else:
                        signal(ins, fin_v, 2 * t + 1)
                r = ss[0:m, 12 + t:13 + t]
                dve.wait_ge(fin_ss, t + 1)
                signal(ts(r, r, 1.0 / D, ALU.mult, EPS, ALU.add), fin_v, 2 * t + 2)
                dve.wait_ge(fin_s, t + 1)
                step(dve.reciprocal(r, r))
                signal(stt(x1[0:m, t, :], x1[0:m, t, :], r, g_fin_b[0:m, :], ALU.mult, ALU.mult), fin_out, t + 1)

        @block.gpsimd
        def _(pool):
            pool.memset(u_pad[:, :, 67:70], 0.0).then_inc(pad_set, 1)
            zero = r_c[0:BLK, 3084:3084 + D]
            pool.memset(zero, 0.0).then_inc(zero_set, 1)
            pool.wait_ge(zero_set, 1)
            pool.dma_start(y_rows_dram[NE * BLK:MAXB * BLK, :].rearrange("(b s) d -> s b d", s=BLK),
                           zero.unsqueeze(1).broadcast_to([BLK, MAXB - NE, D])).then_inc(rows_zeroed, 16)
            filled(pool, "xT", 2, 1)
            ones = vrow.rearrange("p c (h e) -> p c h e", h=4)[:, :, :, 256]
            pool.memset(ones, 1.0).then_inc(ones_set, 1)
            for n in range(16):
                taken(pool, "qk", n)
                pool.tensor_copy(tail[:, 0, :, n], u_pad[:, n % 2, 64:67])
                pool.tensor_copy(tail[:, 1, :, n], u_pad[:, n % 2, 339:342]).then_inc(tail_done, 1)

            def store(dst, src, s=stored):
                pool.dma_start(dst, src).then_inc(s, 16)

            for t, (c0, m) in enumerate(KEYS):
                taken(pool, "kvrow", t)
                if t < 3:
                    store(o["p_lat"][0, 0, c0 - TS:c0 - TS + m, :], kvrow[0:m, t, 0:256])
                    store(o["p_kr"][0, 0, c0 - TS:c0 - TS + m, :], kvrow[0:m, t, 256:320])
                else:
                    store(o["s_lat"][0, 0], kvrow[0:m, t, 0:256])
                    store(o["s_kr"][0, 0], kvrow[0:m, t, 256:320])
            taken(pool, "convrow")
            for w, name in enumerate(("s_conv", "p_conv")):
                store(o[name][0, 0].rearrange("j (c p) -> (j c) p", p=128), tailrow[48 * w:48 * w + 48, :])
            pool.wait_ge(gates_x, 1)
            for w, name in enumerate(("s_m", "p_m")):
                pool.dma_start(o[name][0].rearrange("b h -> h b"), mst[:, 8 - 2 * w:9 - 2 * w],
                               allow_slow_non_contiguous=True).then_inc(stored, 16)
            for c, w in ((0, "s"), (5, "p")):
                for n in range(8):
                    taken(pool, "upd", c, n)
                store(o[w + "_C"][0, 0].rearrange("h (b p) e -> p (h b) e", p=128), C[:, :, 0:256], stored_c)
                taken(pool, "nT", c)
                store(o[w + "_n"][0, 0].rearrange("h (b p) -> (h b) p", p=128), nrow[:, c // 5, :])

            pool.wait_ge(moe_tab, 1)
            nb = pool.value_load(nbi[0:1, 0:1].bitcast(I32), min_val=NE, max_val=MAXB)
            pool.wait_ge(rows_zeroed, 16)
            pool.sem_inc(yrow_free, 1)
            with pool.Fori(0, nb) as b:
                dst = y_rows_dram[bass.ds(pool.snap(b * BLK), BLK), :]
                pool.wait_ge(m_yrow, b + 1)
                pool.wait_ge(moe_tab, 1)
                pool.dma_start(dst, yrow).then_inc(m_store, 16)
                pool.wait_ge(m_store, 16 * b + 16)
                pool.sem_inc(yrow_free, 1)
            pool.wait_ge(m_store, 16 * nb)
            word = u_pad[0:1, 0, 67:68]
            pool.tensor_tensor(word, word, word, ALU.add).then_inc(blocks_out, 1)
            pool.wait_ge(blocks_out, 1)
            pool.wait_ge(desti_set, 3)
            for t, (_, m) in enumerate(ROWS):
                for k in range(4):
                    pool.indirect_dma_start(
                        ring[0:m, (4 * t + k) * D:(4 * t + k + 1) * D], None, y_rows_dram[:, :],
                        bass.IndirectOffsetOnAxis(ap=desti[0:m, t, k:k + 1].bitcast(U32), axis=0)
                    ).then_inc(fin_y[t], 16)
            for t in range(3):
                pool.wait_ge(fin_out, t + 1)
                if t == 0:
                    store(o["y_s"][0], x1[0:64, 0, :])
                    store(o["y_p"][0, 0:48, :], x1[80:128, 0, :])
                elif t == 1:
                    store(o["y_p"][0, 48:176, :], x1[:, 1, :])
                else:
                    store(o["y_p"][0, 176:256, :], x1[0:80, 2, :])
            pool.wait_ge(stored, 16 * 18)
            pool.wait_ge(stored_c, 32)


INS = ["x_prompt", "x_sample", "cache_kv_latent", "cache_k_rope", "state_mlstm_C", "state_mlstm_n", "state_mlstm_m",
       "state_conv", "meta_tokens", "g_mix_norm", "w_in", "b_if", "w_conv", "b_conv", "g_mh_norm", "w_proj_a",
       "g_q_norm", "g_kv_norm", "w_uq", "w_uk", "w_uv", "w_proj_b", "w_out", "g_ffn_norm", "w_router", "b_router",
       "w_gate_up", "b_gate_up", "w_down", "b_down", "g_final_norm"]
OUTS = [("y_p", (1, TX, D)), ("y_s", (1, TS, D)), ("p_lat", (1, 1, TP, KVL)), ("p_kr", (1, 1, TP, ROPE)),
        ("p_C", (1, 1, 4, 256, 256)), ("p_n", (1, 1, 4, 256)), ("p_m", (1, 1, 4)), ("p_conv", (1, 1, 3, 2048)),
        ("s_lat", (1, 1, TS, KVL)), ("s_kr", (1, 1, TS, ROPE)), ("s_C", (1, 1, 4, 256, 256)), ("s_n", (1, 1, 4, 256)),
        ("s_m", (1, 1, 4)), ("s_conv", (1, 1, 3, 2048))]


def kernel(**inputs):
    import concourse.bacc as bacc
    from concourse.bass_utils import run_bass_kernel_spmd as run

    nc = bacc.Bacc("TRN2", target_bir_lowering=False, num_devices=1)
    arrays, i, o = {}, {}, {}
    for name in INS:
        arrays["in_" + name] = np.ascontiguousarray(inputs[name])
    arrays["in_consts"] = constants()
    for name, a in arrays.items():
        i[name[3:]] = nc.dram_tensor(name, a.shape, F32, kind="ExternalInput").ap()
    for name, shape in OUTS:
        o[name] = nc.dram_tensor("out_" + name, shape, F32, kind="ExternalOutput").ap()
    y_rows_dram = nc.dram_tensor("y_rows", (MAXB * BLK, D), F32).ap()
    build(nc, i, o, y_rows_dram)
    r = run(nc, [arrays], core_ids=[0])
    return tuple(r.results[0]["out_" + name] for name, _ in OUTS)
```

```python
import concourse.bass as bass
import numpy as np
from concourse import mybir
from contextlib import ExitStack

F32 = mybir.dt.float32
I32 = mybir.dt.int32
U32 = mybir.dt.uint32
ALU = mybir.AluOpType
ACT = mybir.ActivationFunctionType
AX = mybir.AxisListType

D = 1024
KD = D // 128
TS, TM, TX = 64, 16, 256
TP = TM + TX
NT = TS + TP
PAST = 512
ROWS = [(0, 128), (128, 128), (256, NT - 256)]
CHUNKS = [(0, 64), (64, 16)] + [(80 + 64 * c, 64) for c in range(4)]
KEYS = [(64, 128), (192, 128), (320, 16), (0, 64)]
MH, AH = 4, 8
NOPE, ROPE, KVL, QL = 128, 64, 256, 384
NE, TOPK, BLK = 32, 4, 128
MAXB = NE + NT * TOPK // BLK
NB1 = MAXB + 2
SCALE = float(np.float32((NOPE + ROPE) ** -0.5))
EPS = 1e-6
LIMIT, ALPHA = 7.0, 1.702
NEG = -1e30

CONST_AT = {}
_at = 0
for _name, _n in [("ident", 128), ("ones", 128), ("below", 128), ("cos", NT), ("sin", NT), ("swap", 64),
                  ("mask", NT), ("sel", 4 * 128), ("expert", NE), ("block", NB1)]:
    CONST_AT[_name] = (_at, _n)
    _at += _n
CONST_N = _at


def constants():
    c = np.zeros((128, CONST_N), np.float32)

    def put(name, a):
        o, n = CONST_AT[name]
        c[:a.shape[0], o:o + n] = a

    put("ident", np.eye(128))
    put("ones", np.ones((128, 128)))
    put("below", np.triu(np.ones((128, 128)), 1))
    half = ROPE // 2
    pos = np.concatenate([TM + PAST + np.arange(TS), np.arange(TP)]).astype(np.float32)
    freq = np.float32(10000.0) ** (-np.arange(half, dtype=np.float32) / np.float32(half))
    ang = (pos[None, :] * freq[:, None].astype(np.float32)).astype(np.float32)
    put("cos", np.concatenate([np.cos(ang), np.cos(ang)]))
    put("sin", np.concatenate([-np.sin(ang), np.sin(ang)]))
    put("swap", np.roll(np.eye(ROPE), half, axis=0))
    mask = np.zeros((64, NT))
    for c0, n in CHUNKS:
        mask[:, c0:c0 + n] = np.where(np.arange(64)[:, None] <= np.arange(n)[None, :], 0.0, NEG)
    put("mask", mask)
    sel = np.zeros((4, 4, 128))
    for h in range(4):
        sel[h, h] = 1
    put("sel", sel.reshape(4, 512))
    put("expert", np.tile(np.arange(NE), (128, 1)))
    put("block", np.tile(np.arange(NB1), (128, 1)))
    return c


PANELS = (["ifq", "kv"] + [f"qk{i}" for i in range(4)] + ["v0", "v1", "o0", "o1", "uq0", "uq1", "ukuv"]
          + [f"g{i}" for i in range(4)] + ["pa0", "pa1", "pb0", "pb1", "wo0", "wo1"])
SLOT = 4096
UPSLOT, DNSLOT = [4, 5, 3, 0], [1, 2]


def by_chunk(pair, h, src):
    return [(pair[:, TS * h:TS * h + TS], src[:, 0:TS]),
            (pair[:, 2 * TS + TM * h:2 * TS + TM * h + TM], src[:, TS:TS + TM]),
            (pair[:, 2 * (TS + TM):2 * NT].rearrange("p (c h t) -> p c h t", c=4, h=2)[:, :, h, :],
             src[:, TS + TM:NT].rearrange("p (c t) -> p c t", c=4))]


def units(hp):
    return [(hp, c) for c in range(6)]


def job_list():
    j = [("vecT",), ("convT",), ("buT",)]
    j += [("xT", t, s) for t in range(3) for s in range(2)]
    j += [("ig",), ("fg",)] + [("cq", i) for i in range(3)]
    j += [("ckv", 0), ("ckv", 1), ("kr",), ("ssq",), ("ssk",), ("krs",)]
    j += [("qk", i) for i in range(8)]
    j += [("kvrow", t) for t in range(4)]
    j += [("qk", i) for i in range(8, 16)]
    j += [("wi", h) for h in range(4)] + [("mx", h) for h in range(4)] + [("cols",)]
    j += [("v", i) for i in range(8)] + [("convrow",)]
    j += [("o", i) for i in range(8)]
    for c in range(6):
        j += [("krow", c, s) for s in range(2)] + [("vrow", c, s) for s in range(2)] + [("s", c)]
        j += [("num", c, h) for h in range(4)]
        j += [("upd", c, i) for i in range(8)]
        if c in (0, 5):
            j += [("nT", c)]
        if c:
            j += [("hT", c - 1)]
    j += [("hT", 5)]
    j += [("cacheT", t) for t in range(4)]
    for hp in range(4):
        j += [("ukT", hp)]
        for h in (0, 1):
            j += [("qn", hp, h), ("qr", hp, h), ("qrs", hp, h)]
        j += [("ql", hp, i) for i in range(4)]
        u = units(hp)
        for n in range(len(u) + 2):
            if n < len(u):
                j += [("sc",) + u[n] + (p,) for p in range(2 if u[n][1] == 0 else 1)]
            if n >= 2:
                j += [("ol",) + u[n - 2]]
            if 1 <= n <= len(u):
                j += [("pT",) + u[n - 1] + (p,) for p in range(2 if u[n - 1][1] == 0 else 1)]
        j += [("ov", hp, h) for h in (0, 1)]
    j += [("g", i) for i in range(16)]
    j += [("ya", i) for i in range(8)] + [("yb", i) for i in range(8)]
    j += [("out", t, s) for t in range(3) for s in range(2)]
    j += [("x2T", t, s) for t in range(3) for s in range(2)]
    j += [("lg", t) for t in range(3)] + [("pos", t) for t in range(3)] + [("cnt",)]
    j += [("gT", t) for t in range(3)] + [("bd", t, s) for t in range(3) for s in range(2)]
    return j


JOBS = job_list()
JOB = {name: n for n, name in enumerate(JOBS)}
assert len(JOB) == len(JOBS)


def qcol(col):
    return col if col < TS else col + 3


def build(nc, i, o, x_rows_dram, y_rows_dram):
    with ExitStack() as ctx:
        def sb(name, shape, dt=F32):
            return ctx.enter_context(nc.sbuf_tensor(name, shape, dt))

        def sem(name):
            return ctx.enter_context(nc.semaphore(name))

        ring = sb("ring", [128, 6 * SLOT])
        r_xt = sb("r_xt", [128, KD * NT])
        r_o = sb("r_o", [128, KD * NT])
        r_kv = sb("r_kv", [128, 3968])
        r_qk = sb("r_qk", [128, 16 * (NT + 3)])
        r_v = sb("r_v", [128, KD * NT])
        r_c = sb("r_c", [128, 4112])
        const = sb("const", [128, CONST_N])
        bu_t = sb("bu_t", [128, 16, NE])
        vec_rows = sb("vec_rows", [128, 128])
        conv_rows = sb("conv_rows", [48, 128])
        vec = sb("vec", [128, 112])
        convst = sb("convst", [128, 3, 16])
        b_router_b = sb("b_router_b", [128, NE])
        u_pad = sb("u_pad", [128, 2, NT + 6])
        sig = sb("sig", [128, 2, NT + 3])
        tail = sb("tail", [128, 2, 3, 16])
        tailrow = sb("tailrow", [96, 128])
        ss = sb("ss", [128, 16])
        b_if = sb("b_if", [4, 2])
        mst = sb("mst", [4, 16])
        wprev = sb("wprev", [128, 4, 6])
        colT = sb("colT", [64, 6, 3, 4])
        hs = sb("hs", [64, 8, 4])
        nrow = sb("nrow", [8, 2, 128])
        st = sb("st", [128, 2, 8])

        def cst(name, rows=128):
            at, n = CONST_AT[name]
            return const[0:rows, at:at + n]

        def r3(ap, a):
            return ap.rearrange("p (a b) -> p a b", a=a)

        ident = cst("ident")
        scratch = ring[:, 4 * SLOT:6 * SLOT]

        x_rows = r3(scratch[:, 0:3072], 3)
        xn_rows = r3(scratch[:, 3072:6144], 3)
        bu_rows = r_qk[0:NE, 0:2048]
        bd_rows = r_kv[0:NE, 1024:2048]
        xT = r3(r_xt[:, :], KD)
        qk = r3(r_qk[:, :], 16)
        vT = r3(r_v[:, :], KD)
        oT = r3(r_o[:, :], KD)
        cq = r3(r_kv[:, 0:1008], 3)
        lat = r3(r_kv[:, 1008:1680], 2)
        krT = r_kv[0:64, 1680:2016]
        kvrow = r3(r_kv[:, 2016:3296], 4)
        rq = r_kv[:, 3296:3632]
        rk = r_kv[:, 3632:3968]
        sq = r3(r_v[:, 0:5 * NT], 5)
        kr_raw = r_v[0:64, 5 * NT:6 * NT]
        kr_tmp = r_v[0:64, 6 * NT:7 * NT]
        rows4 = r3(r_o[0:4, :], 8)
        R_IG, R_LF, R_B, R_A, R_MX, R_WI, R_DN, R_WK = (rows4[:, n, :] for n in range(8))
        krow = r3(scratch[0:64, 0:2048], 2)
        vrow = r3(scratch[0:64, 2048:4104], 2)
        emat = r3(scratch[0:64, 4104:5448], 4)
        wib = r3(scratch[:, 5448:6792], 4)
        sT = r3(scratch[0:64, 6792:7048], 4)
        junk = scratch[0:64, 7048:7304]
        wexp = r3(scratch[0:64, 7304:7560], 4)
        C = r3(r_c[:, 0:2056], 8)
        num = r_c[0:64, 2056:4112].rearrange("p (b h e) -> p b h e", b=2, h=4)
        qn = r3(scratch[:, 0:672], 2)
        qlat = r3(scratch[:, 672:2016], 2)
        qr = scratch[0:64, 2016:2688]
        qx = r3(scratch[0:64, 2688:3360], 2)
        olat = scratch[:, 3360:4704].rearrange("p (r h t) -> p r h t", r=2, h=2)
        prob = r3(scratch[:, 4704:5856], 2)
        pT = scratch[:, 5856:7136].rearrange("p (b k q) -> p b k q", b=2, k=5)
        ukT = scratch[:, 7136:7648].rearrange("p (h r) -> p h r", h=2)
        qtmp = scratch[0:64, 7648:7984]
        cache_row = r3(r_c[:, 0:1280], 4)
        cache_lat = r3(r_c[:, 1280:2304], 2)
        cache_kr = r_c[0:64, 2304:2816]
        ovT = r3(r_v[:, :], KD)
        gates = r3(r_qk[:, 0:16 * NT], 16)
        mixed = r3(r_xt[:, :], KD)
        x1 = r3(r_c[:, 0:3072], 3)
        x2 = r3(r_qk[:, 0:3072], 3)
        x2T = r3(r_o[:, :], KD)
        g_ffn_b = r_v[:, 1216:2240]
        g_fin_b = r_xt[:, 0:1024]
        w_rt = r3(r_xt[:, 1024:1280], KD)

        tab_at = [3072]

        def small(n, rows=128):
            a = tab_at[0]
            tab_at[0] += n
            assert tab_at[0] <= 16 * (NT + 3)
            return r_qk[0:rows, a:a + n]

        logit = r3(small(3 * NE), 3)
        top = r3(small(24), 3)
        topi = r3(small(24), 3)
        topif = r3(small(24), 3)
        onehot = small(12 * NE).rearrange("p (t k e) -> p t k e", t=3, k=4)
        chosen = r3(small(3 * NE), 3)
        gate = r3(small(24), 3)
        gsum = small(8)
        posm = r3(small(3 * NE), 3)
        gmat = r3(small(3 * NE), 3)
        dest = r3(small(12), 3)
        desti = r3(small(12), 3)
        nblk = small(NE)
        pend = small(NE)
        start = small(NE)
        t32 = small(NE)
        be = small(NB1)
        bei = small(NB1)
        nbi = small(2)

        xg = r3(r_kv[:, 0:1024], 8)
        gt = r3(r_kv[:, 1024:2048], 8)
        up = r3(r_kv[:, 2048:3072], 8)
        sg = r3(r_o[:, 0:1024], 8)
        gateT = r_o[0:NE, 1024:1024 + NT]
        hid = r3(r_v[:, 0:1024], 8)
        xrow = r_v[:, 1216:2240]
        yrow = r_xt[:, 1280:2304]

        def up_w(c):
            return ring[:, UPSLOT[c] * SLOT:(UPSLOT[c] + 1) * SLOT].rearrange("p (k f) -> p k f", k=8)

        def up_at(c):
            return slice(D * (c % 2) + 512 * (c // 2), D * (c % 2) + 512 * (c // 2) + 512)

        def dn_w(c):
            return ring[:, DNSLOT[c] * SLOT:(DNSLOT[c] + 1) * SLOT].rearrange("p (k f) -> p k f", k=4)

        V_GMIX, V_BCONV, V_WCONV, V_GMH, V_GQ, V_GKV, V_N0 = 0, 8, 24, 88, 96, 99, 101
        NVEC = 109

        banks = [ctx.enter_context(nc.psum_tensor(f"bank{b}", [128, 512], F32)) for b in range(8)]
        bank_full = [sem(f"bank_full{b}") for b in range(8)]
        bank_free = [sem(f"bank_free{b}") for b in range(8)]

        def bank(name):
            return banks[JOB[name] % 8]

        def filled(eng, *name):
            n = JOB[name]
            eng.wait_ge(bank_full[n % 8], n // 8 + 1)

        def taken(eng, *name):
            n = JOB[name]
            eng.wait_ge(bank_free[n % 8], n // 8 + 1)

        ld_const, ld_vec, ld_x, ld_mem, ld_be, ld_late = map(sem, (
            "ld_const", "ld_vec", "ld_x", "ld_mem", "ld_be", "ld_late"))
        ld_cache, ld_x1 = sem("ld_cache"), sem("ld_x1")
        slot_in = [sem(f"slot_in{n}") for n in range(4)]
        chunk_in = [sem(f"chunk_in{n}") for n in range(6)]
        (rms_v, rms_s, xn_ready, cq_ready, kv_ready, kr_ready, low_v, low_s, conv_done, sig_ready, qk_ready,
         tail_done, pad_set, ones_set, n_set, lg_d, lg_a, gates_x, gates4, wprev_ready, e_ready, q_scaled, hs_v, hs_s,
         hn_ready, q_ready, pmax, pnorm, mix_a, x1_ss, x1_v, x1_s, x2_ready, chosen_set, gate_x, gate_e, moe_tab,
         stored, stored_c) = map(sem, (
             "rms_v", "rms_s", "xn_ready", "cq_ready", "kv_ready", "kr_ready", "low_v", "low_s", "conv_done",
             "sig_ready", "qk_ready", "tail_done", "pad_set", "ones_set", "n_set", "lg_d", "lg_a", "gates_x", "gates4",
             "wprev_ready", "e_ready", "q_scaled", "hs_v", "hs_s", "hn_ready", "q_ready", "pmax", "pnorm", "mix_a",
             "x1_ss", "x1_v", "x1_s", "x2_ready", "chosen_set", "gate_x", "gate_e", "moe_tab", "stored", "stored_c"))
        m_glu, gates_set = sem("m_glu"), sem("gates_set")
        (m_xrow, m_gath, m_xg, m_gt, m_sig, m_hid, m_yrow, m_used, m_store, m_dve, m_act,
         fin_v, fin_ss, fin_s, fin_out, all_out) = map(sem, (
             "m_xrow", "m_gath", "m_xg", "m_gt", "m_sig", "m_hid", "m_yrow", "m_used", "m_store",
             "m_dve", "m_act", "fin_v", "fin_ss", "fin_s", "fin_out", "all_out"))
        desti_set, blocks_out, x_sent = sem("desti_set"), sem("blocks_out"), sem("x_sent")
        yrow_free, zero_set, rows_zeroed = sem("yrow_free"), sem("zero_set"), sem("rows_zeroed")
        fin_y = [sem(f"fin_y{t}") for t in range(3)]
        dve_step, act_step = sem("dve_step"), sem("act_step")

        def pslot(p, n):
            return ring[:, (p % 4) * SLOT:(p % 4) * SLOT + n]

        w_in = i["w_in"][0].rearrange("(k p) c -> p k c", p=128)
        sq_w = {n: i[w][0].rearrange("(k p) c -> p k c", p=128)
                for n, w in (("pa", "w_proj_a"), ("pb", "w_proj_b"), ("wo", "w_out"))}
        in_at = {"ifq": (4096, 392), "kv": (4488, 320)}
        for n in range(4):
            in_at[f"qk{n}"] = (512 * n, 512)
            in_at[f"g{n}"] = (4808 + 512 * n, 512)
        for n in range(2):
            in_at[f"v{n}"] = (2048 + 512 * n, 512)
            in_at[f"o{n}"] = (3072 + 512 * n, 512)
        PV, loads, need = {}, {}, {}
        slot_sum = [0] * 4
        for p, name in enumerate(PANELS):
            if name in in_at:
                at, n = in_at[name]
                PV[name] = r3(pslot(p, 8 * n), 8)
                loads[name] = [(PV[name], w_in[:, :, at:at + n])]
            elif name[:2] in sq_w:
                PV[name] = r3(pslot(p, 4096), 8)
                c = int(name[2])
                loads[name] = [(PV[name], sq_w[name[:2]][:, :, 512 * c:512 * c + 512])]
            elif name[:2] == "uq":
                PV[name] = r3(pslot(p, 3 * 768), 3)
                c = int(name[2])
                loads[name] = [(PV[name], i["w_uq"][0].rearrange("(k p) c -> p k c", p=128)[
                    :, :, 768 * c:768 * c + 768])]
            else:
                v = pslot(p, 4096)
                PV["uk"], PV["uv"] = r3(v[:, 0:2048], 2), r3(v[:, 2048:4096], 2)
                loads[name] = [(PV[w], i["w_" + w][0].rearrange("(k p) h n -> p k (h n)", p=128))
                               for w in ("uk", "uv")]
            slot_sum[p % 4] += 16 * len(loads[name])
            need[name] = slot_sum[p % 4]
        last_job = {"ifq": ("cq", 2), "kv": ("kr",), "uq0": ("qr", 1, 1), "uq1": ("qr", 3, 1), "ukuv": ("ov", 3, 1)}
        for n in range(4):
            last_job[f"qk{n}"] = ("qk", 4 * n + 3)
            last_job[f"g{n}"] = ("g", 4 * n + 3)
        for n in range(2):
            last_job[f"v{n}"] = ("v", 4 * n + 3)
            last_job[f"o{n}"] = ("o", 4 * n + 3)
            last_job[f"pa{n}"] = ("ya", 4 * n + 3)
            last_job[f"pb{n}"] = ("yb", 4 * n + 3)
            last_job[f"wo{n}"] = ("out", 2, n)

        def panel_here(eng, name):
            eng.wait_ge(slot_in[PANELS.index(name) % 4], need[name])

        gu = i["w_gate_up"][0].rearrange("e (k p) f -> p e k f", p=128)
        dn = i["w_down"][0].rearrange("e (k p) f -> p e k f", p=128)

        block = ctx.enter_context(nc.Block())

        @block.sync
        def _(sp):
            sp.dma_start(x_rows[0:64, 0, :], i["x_sample"][0]).then_inc(ld_x, 16)
            sp.dma_start(x_rows[64:80, 0, :], i["meta_tokens"]).then_inc(ld_x, 16)
            sp.dma_start(x_rows[80:128, 0, :], i["x_prompt"][0, 0:48, :]).then_inc(ld_x, 16)
            sp.dma_start(x_rows[:, 1, :], i["x_prompt"][0, 48:176, :]).then_inc(ld_x, 16)
            sp.dma_start(x_rows[0:80, 2, :], i["x_prompt"][0, 176:256, :]).then_inc(ld_x, 16)
            sp.dma_start(const[:, :], i["consts"]).then_inc(ld_const, 16)
            at = 0
            for name, n in (("g_mix_norm", 8), ("b_conv", 16), ("w_conv", 64), ("g_mh_norm", 8), ("g_q_norm", 3),
                            ("g_kv_norm", 2), ("state_mlstm_n", 8)):
                flat = i[name].rearrange({2: "a b -> (a b)", 3: "a b c -> (a b c)", 4: "a b c d -> (a b c d)"}[
                    len(i[name].shape)])
                sp.dma_start(vec_rows[at:at + n, :], flat.rearrange("(a b) -> a b", b=128)).then_inc(ld_vec, 16)
                at += n
            sp.dma_start(conv_rows[:, :], i["state_conv"].rearrange("a b j (c p) -> (a b j c) p", p=128)
                         ).then_inc(ld_vec, 16)
            sp.dma_start(bu_rows, i["b_gate_up"][0]).then_inc(ld_vec, 16)
            for n in range(4):
                for dst, src in loads[PANELS[n]]:
                    sp.dma_start(dst, src).then_inc(slot_in[n], 16)
            sp.dma_start(b_if[:, :], i["b_if"].rearrange("a (j h) -> h (a j)", h=4),
                         allow_slow_non_contiguous=True).then_inc(ld_mem, 16)
            sp.dma_start(mst[:, 0:1], i["state_mlstm_m"].rearrange("a b h -> h (a b)"),
                         allow_slow_non_contiguous=True).then_inc(ld_mem, 16)
            sp.dma_start(C[:, :, 0:256], i["state_mlstm_C"][0, 0].rearrange("h (b p) e -> p (h b) e", p=128)
                         ).then_inc(ld_mem, 16)
            sp.dma_start(b_router_b[:, :], i["b_router"].broadcast_to([128, NE])).then_inc(ld_mem, 16)
            for p in range(4, len(PANELS)):
                filled(sp, *last_job[PANELS[p - 4]])
                for dst, src in loads[PANELS[p]]:
                    sp.dma_start(dst, src).then_inc(slot_in[p % 4], 16)
                if PANELS[p] == "g0":
                    sp.wait_ge(stored_c, 32)
                    filled(sp, "hT", 5)
                    sp.dma_start(cache_row[:, :, 0:256], i["cache_kv_latent"][0, 0].rearrange("(t p) r -> p t r", p=128)
                                 ).then_inc(ld_cache, 16)
                    sp.dma_start(cache_row[:, :, 256:320], i["cache_k_rope"][0, 0].rearrange("(t p) r -> p t r", p=128)
                                 ).then_inc(ld_cache, 16)
            filled(sp, "ov", 3, 1)
            sp.dma_start(x1[0:64, 0, :], i["x_sample"][0]).then_inc(ld_x1, 16)
            sp.dma_start(x1[64:80, 0, :], i["meta_tokens"]).then_inc(ld_x1, 16)
            sp.dma_start(x1[80:128, 0, :], i["x_prompt"][0, 0:48, :]).then_inc(ld_x1, 16)
            sp.dma_start(x1[:, 1, :], i["x_prompt"][0, 48:176, :]).then_inc(ld_x1, 16)
            sp.dma_start(x1[0:80, 2, :], i["x_prompt"][0, 176:256, :]).then_inc(ld_x1, 16)
            sp.dma_start(up_w(0), gu[:, 0, :, up_at(0)]).then_inc(chunk_in[0], 16)
            sp.dma_start(up_w(1), gu[:, 0, :, up_at(1)]).then_inc(chunk_in[1], 16)
            filled(sp, "yb", 7)
            sp.dma_start(g_ffn_b, i["g_ffn_norm"].broadcast_to([128, D])).then_inc(ld_late, 16)
            sp.dma_start(up_w(2), gu[:, 0, :, up_at(2)]).then_inc(chunk_in[2], 16)
            sp.dma_start(up_w(3), gu[:, 0, :, up_at(3)]).then_inc(chunk_in[3], 16)
            sp.wait_ge(stored, 16 * 14)
            sp.dma_start(bd_rows, i["b_down"][0]).then_inc(ld_late, 16)
            filled(sp, "out", 2, 0)
            filled(sp, "out", 2, 1)
            sp.dma_start(w_rt, i["w_router"][0].rearrange("(k p) e -> p k e", p=128)).then_inc(ld_late, 16)
            sp.dma_start(g_fin_b, i["g_final_norm"].rearrange("(a d) -> a d", a=1).broadcast_to([128, D])
                         ).then_inc(ld_late, 16)
            sp.dma_start(dn_w(0), dn[:, 0, 0:4, :]).then_inc(chunk_in[4], 16)
            sp.dma_start(dn_w(1), dn[:, 0, 4:8, :]).then_inc(chunk_in[5], 16)
            sp.wait_ge(x_sent, 16 * 12)
            sp.dma_start(xrow, x_rows_dram[0:BLK, :]).then_inc(m_xrow, 16)
            sp.wait_ge(moe_tab, 1)
            nb = sp.value_load(nbi[0:1, 0:1].bitcast(I32), min_val=NE, max_val=MAXB)
            with sp.Fori(1, nb) as b:
                src = x_rows_dram[bass.ds(sp.snap(b * BLK), BLK), :]
                sp.wait_ge(m_gath, b)
                sp.dma_start(xrow, src).then_inc(m_xrow, 16)
                e = sp.value_load(bei[0:1, bass.ds(b, 1)].bitcast(I32), min_val=0, max_val=NE - 1)
                for c in range(6):
                    dst = up_w(c) if c < 4 else dn_w(c - 4)
                    src = gu[:, bass.ds(e, 1), :, up_at(c)] if c < 4 else \
                        dn[:, bass.ds(e, 1), 4 * (c - 4):4 * (c - 4) + 4, :]
                    sp.wait_ge(m_used, (b - 1) * 6 + c + 1)
                    sp.dma_start(dst, src.rearrange("p a k f -> p (a k) f")).then_inc(chunk_in[c], 16)
            src = x_rows_dram[bass.ds(sp.snap(nb * BLK), BLK), :]
            sp.wait_ge(m_gath, nb)
            sp.dma_start(xrow, src).then_inc(m_xrow, 16)

        @block.tensor
        def _(pe):
            def begin(*name):
                n = JOB[name]
                if n >= 8:
                    pe.wait_ge(bank_free[n % 8], n // 8)
                return banks[n % 8]

            def end(ins, *name):
                ins.then_inc(bank_full[JOB[name] % 8], 1)

            def group(out, pairs, **kw):
                for n, (l, r) in enumerate(pairs):
                    ins = pe.matmul(out, l, r, start=(n == 0), stop=(n == len(pairs) - 1), **kw)
                return ins

            def turn(out, src):
                return pe.transpose(out, src, ident[0:src.shape[0], 0:src.shape[0]])

            pe.wait_ge(ld_const, 16)
            pe.wait_ge(ld_vec, 144)
            b = begin("vecT")
            end(turn(b[:, 0:NVEC], vec_rows[0:NVEC, :]), "vecT")
            b = begin("convT")
            end(turn(b[:, 0:48], conv_rows[:, :]), "convT")
            b = begin("buT")
            for n in range(16):
                ins = turn(b[:, 32 * n:32 * n + 32], bu_rows[:, 128 * n:128 * n + 128])
            end(ins, "buT")
            for t, (c0, n) in enumerate(ROWS):
                pe.wait_ge(xn_ready, t + 1)
                for s in range(2):
                    b = begin("xT", t, s)
                    for k in range(4):
                        ins = turn(b[:, n * k:n * k + n], xn_rows[0:n, t, 128 * (4 * s + k):128 * (4 * s + k) + 128])
                    end(ins, "xT", t, s)

            def project(name, panel, at, m, src=xT, kk=KD):
                b = begin(*name)
                end(group(b[0:m, 0:NT], [(PV[panel][:, k, at:at + m], src[:, k, :]) for k in range(kk)]), *name)

            for t in range(3):
                for s in range(2):
                    taken(pe, "xT", t, s)
            panel_here(pe, "ifq")
            project(("ig",), "ifq", 0, 4)
            project(("fg",), "ifq", 4, 4)
            for n in range(3):
                project(("cq", n), "ifq", 8 + 128 * n, 128)
            panel_here(pe, "kv")
            for n in range(2):
                project(("ckv", n), "kv", 128 * n, 128)
            project(("kr",), "kv", 256, 64)
            for name, lo, hi in (("ssq", 0, 3), ("ssk", 3, 5)):
                pe.wait_ge(cq_ready, hi)
                b = begin(name)
                end(group(b[:, 0:NT], [(cst("ones"), sq[:, k, :]) for k in range(lo, hi)]), name)
            taken(pe, "kr")
            b = begin("krs")
            end(group(b[0:64, 0:NT], [(cst("swap", 64), kr_raw)]), "krs")
            for n in range(16):
                if n == 8:
                    pe.wait_ge(kv_ready, 2)
                    pe.wait_ge(kr_ready, 1)
                    for t, (c0, m) in enumerate(KEYS):
                        b = begin("kvrow", t)
                        turn(b[0:m, 0:128], lat[:, 0, c0:c0 + m])
                        turn(b[0:m, 128:256], lat[:, 1, c0:c0 + m])
                        end(turn(b[0:m, 256:320], krT[:, c0:c0 + m]), "kvrow", t)
                panel_here(pe, f"qk{n // 4}")
                project(("qk", n), f"qk{n // 4}", 128 * (n % 4), 128)
            pe.wait_ge(gates4, 1)
            for h in range(4):
                b = begin("wi", h)
                end(group(b[:, 0:NT], [(cst("sel", 4)[:, 128 * h:128 * h + 128], R_WI)]), "wi", h)
            for h in range(4):
                b = begin("mx", h)
                end(group(b[0:64, 0:NT], [(cst("sel", 4)[:, 128 * h:128 * h + 64], R_MX)]), "mx", h)
            b = begin("cols")
            for c, (c0, m) in enumerate(CHUNKS):
                for q, row in enumerate((R_A, R_DN, R_WK)):
                    at = 12 * c + 4 * q
                    ins = turn(b[0:m, at:at + 4], row[:, c0:c0 + m])
            end(ins, "cols")
            for n in range(8):
                panel_here(pe, f"v{n // 4}")
                project(("v", n), f"v{n // 4}", 128 * (n % 4), 128)
            pe.wait_ge(tail_done, 16)
            b = begin("convrow")
            end(turn(b[0:96, 0:128], tail[:, :, :, :].rearrange("p a b c -> p (a b c)")), "convrow")
            for n in range(8):
                panel_here(pe, f"o{n // 4}")
                project(("o", n), f"o{n // 4}", 128 * (n % 4), 128)

            for n in range(8):
                taken(pe, "v", n)
            pe.wait_ge(qk_ready, 16)

            def heads_turned(c):
                m = CHUNKS[c][1]
                pe.wait_ge(hn_ready, c + 1)
                b = begin("hT", c)
                for k in range(8):
                    ins = turn(b[:, 64 * k:64 * k + m],
                               num[0:m, c % 2, k // 2, 128 * (k % 2):128 * (k % 2) + 128])
                end(ins, "hT", c)

            for c, (c0, m) in enumerate(CHUNKS):
                q0 = qcol(c0)
                for s in range(2):
                    b = begin("krow", c, s)
                    for k in range(4):
                        ins = turn(b[0:m, 128 * k:128 * k + 128], qk[:, 8 + 4 * s + k, q0:q0 + m])
                    end(ins, "krow", c, s)
                for s in range(2):
                    b = begin("vrow", c, s)
                    for k in range(4):
                        ins = turn(b[0:m, 128 * k:128 * k + 128], vT[:, 4 * s + k, c0:c0 + m])
                    end(ins, "vrow", c, s)
                b = begin("s", c)
                for h in range(4):
                    ins = group(b[0:m, 64 * h:64 * h + m],
                                [(qk[:, 8 + 2 * h + j, q0:q0 + m], qk[:, 2 * h + j, q0:q0 + m]) for j in range(2)])
                end(ins, "s", c)
                pe.wait_ge(q_scaled, c + 1)
                taken(pe, "s", c)
                for s in range(2):
                    taken(pe, "krow", c, s)
                    taken(pe, "vrow", c, s)
                if c == 0:
                    pe.wait_ge(ones_set, 1)
                    pe.wait_ge(ld_mem, 64)
                    pe.wait_ge(n_set, 1)
                else:
                    for n in range(8):
                        taken(pe, "upd", c - 1, n)
                for h in range(4):
                    b = begin("num", c, h)
                    v = vrow[0:m, c % 2, 257 * h:257 * h + 257]
                    pairs = [(sT[0:m, h, 0:m], v)]
                    if c != 1:
                        pairs += [(qk[:, 2 * h + j, q0:q0 + m], C[:, 2 * h + j, :]) for j in range(2)]
                    end(group(b[0:m, 0:257], pairs), "num", c, h)
                for n in range(8):
                    b = begin("upd", c, n)
                    end(group(b[:, 0:257], [(krow[0:m, c % 2, 128 * n:128 * n + 128],
                                             vrow[0:m, c % 2, 257 * (n // 2):257 * (n // 2) + 257])]), "upd", c, n)
                if c in (0, 5):
                    for n in range(8):
                        taken(pe, "upd", c, n)
                    b = begin("nT", c)
                    end(turn(b[0:8, 0:128], C[:, :, 256]), "nT", c)
                if c:
                    heads_turned(c - 1)
            heads_turned(5)

            pe.wait_ge(ld_cache, 32)
            for t in range(4):
                b = begin("cacheT", t)
                turn(b[:, 0:128], cache_row[:, t, 0:128])
                turn(b[:, 128:256], cache_row[:, t, 128:256])
                end(turn(b[0:64, 256:384], cache_row[:, t, 256:320]), "cacheT", t)
            for t in range(4):
                taken(pe, "cacheT", t)
                taken(pe, "kvrow", t)
            panel_here(pe, "ukuv")
            for hp in range(4):
                b = begin("ukT", hp)
                for h in (0, 1):
                    for r in (0, 1):
                        at = 128 * (2 * hp + h)
                        ins = turn(b[:, 256 * h + 128 * r:256 * h + 128 * r + 128], PV["uk"][:, r, at:at + 128])
                end(ins, "ukT", hp)
                w = f"uq{hp // 2}"
                panel_here(pe, w)
                for h in (0, 1):
                    at = 192 * (2 * (hp % 2) + h)
                    project(("qn", hp, h), w, at, 128, cq, 3)
                    project(("qr", hp, h), w, at + 128, 64, cq, 3)
                    taken(pe, "qr", hp, h)
                    b = begin("qrs", hp, h)
                    end(group(b[0:64, 0:NT], [(cst("swap", 64), qx[:, h, :])]), "qrs", hp, h)
                taken(pe, "ukT", hp)
                for h in (0, 1):
                    taken(pe, "qn", hp, h)
                for n in range(4):
                    h, r = n // 2, n % 2
                    b = begin("ql", hp, n)
                    end(group(b[:, 0:NT], [(ukT[:, h, 128 * r:128 * r + 128], qn[:, h, :])]), "ql", hp, n)
                for n in range(4):
                    taken(pe, "ql", hp, n)
                pe.wait_ge(q_ready, 2 * hp + 2)

                def scores(hp, c):
                    c0, m = CHUNKS[c]
                    ql_ = [qlat[:, r, 2 * c0:2 * c0 + 2 * m] for r in (0, 1)]
                    qr_ = qr[:, 2 * c0:2 * c0 + 2 * m]
                    parts = [(cache_lat, 0, PAST, cache_kr), (lat, 0, TS, krT)] if c == 0 else \
                        [(lat, TS, c0 + m - TS, krT)]
                    for p, (kl, k0, n, kr_) in enumerate(parts):
                        b = begin("sc", hp, c, p)
                        end(group(b[0:2 * m, 0:n], [(ql_[r], kl[:, r, k0:k0 + n]) for r in (0, 1)]
                                  + [(qr_, kr_[:, k0:k0 + n])]), "sc", hp, c, p)

                def key_tiles(c):
                    if c == 0:
                        return [(0, k, 128, cache_row[:, k, :]) for k in range(4)] + [(1, 4, TS, kvrow[:, 3, :])]
                    n = sum(CHUNKS[c]) - TS
                    return [(0, k, min(128, n - 128 * k), kvrow[:, k, :]) for k in range((n + 127) // 128)]

                def turn_probs(hp, c):
                    u, m, sizes = 6 * hp + c, CHUNKS[c][1], key_tiles(c)
                    pr = prob[0:2 * m, u % 2, :]
                    pe.wait_ge(pnorm, u + 1)
                    for p in range(sizes[-1][0] + 1):
                        b = begin("pT", hp, c, p)
                        for pp, k, n, _ in sizes:
                            if pp == p:
                                ins = turn(b[0:n, 128 * (k % 4):128 * (k % 4) + 2 * m], pr[:, 128 * k:128 * k + n])
                        end(ins, "pT", hp, c, p)

                def attend(hp, c):
                    u, m, sizes = 6 * hp + c, CHUNKS[c][1], key_tiles(c)
                    pt = pT[:, u % 2, :, :]
                    for p in range(sizes[-1][0] + 1):
                        taken(pe, "pT", hp, c, p)
                    b = begin("ol", hp, c)
                    for r in (0, 1):
                        ins = group(b[:, 128 * r:128 * r + 2 * m],
                                    [(row[0:n, 128 * r:128 * r + 128], pt[0:n, k, 0:2 * m]) for _, k, n, row in sizes])
                    end(ins, "ol", hp, c)

                for c in range(8):
                    if c < 6:
                        scores(hp, c)
                    if c >= 2:
                        attend(hp, c - 2)
                    if 1 <= c <= 6:
                        turn_probs(hp, c - 1)
                for c in range(6):
                    taken(pe, "ol", hp, c)
                for h in (0, 1):
                    b = begin("ov", hp, h)
                    at = 128 * (2 * hp + h)
                    end(group(b[:, 0:NT], [(PV["uv"][:, r, at:at + 128], olat[:, r, h, :]) for r in (0, 1)]),
                        "ov", hp, h)

            for n in range(16):
                panel_here(pe, f"g{n // 4}")
                project(("g", n), f"g{n // 4}", 128 * (n % 4), 128)
            for c in range(6):
                taken(pe, "hT", c)
            for n in range(8):
                panel_here(pe, f"pa{n // 4}")
                project(("ya", n), f"pa{n // 4}", 128 * (n % 4), 128, oT)
            for hp in range(4):
                for h in (0, 1):
                    taken(pe, "ov", hp, h)
            for n in range(8):
                panel_here(pe, f"pb{n // 4}")
                project(("yb", n), f"pb{n // 4}", 128 * (n % 4), 128, ovT)
            pe.wait_ge(mix_a, 8)
            for t, (c0, m) in enumerate(ROWS):
                for s in range(2):
                    panel_here(pe, f"wo{s}")
                    b = begin("out", t, s)
                    end(group(b[0:m, :], [(mixed[:, k, c0:c0 + m], PV[f"wo{s}"][:, k, :]) for k in range(8)]),
                        "out", t, s)
            for t, (c0, m) in enumerate(ROWS):
                pe.wait_ge(x2_ready, t + 1)
                for s in range(2):
                    b = begin("x2T", t, s)
                    for k in range(4):
                        ins = turn(b[:, m * k:m * k + m], x2[0:m, t, 128 * (4 * s + k):128 * (4 * s + k) + 128])
                    end(ins, "x2T", t, s)
            pe.wait_ge(ld_late, 64)
            for t, (c0, m) in enumerate(ROWS):
                for s in range(2):
                    taken(pe, "x2T", t, s)
                b = begin("lg", t)
                end(group(b[0:m, 0:NE], [(x2T[:, k, c0:c0 + m], w_rt[:, k, :]) for k in range(8)]), "lg", t)
            pe.wait_ge(chosen_set, 3)
            for t, (c0, m) in enumerate(ROWS):
                b = begin("pos", t)
                pairs = [(cst("ones")[0:ROWS[s][1], 0:m], chosen[0:ROWS[s][1], s, :]) for s in range(t)]
                pairs += [(cst("below")[0:m, 0:m], chosen[0:m, t, :])]
                end(group(b[0:m, 0:NE], pairs), "pos", t)
            b = begin("cnt")
            end(group(b[:, 0:NE], [(cst("ones")[0:n, :], chosen[0:n, t, :]) for t, (_, n) in enumerate(ROWS)]), "cnt")

            for t, (c0, m) in enumerate(ROWS):
                pe.wait_ge(gates_set, t + 1)
                b = begin("gT", t)
                end(turn(b[0:NE, 0:m], gmat[0:m, t, :]), "gT", t)
            for t, (c0, m) in enumerate(ROWS):
                taken(pe, "gT", t)
                for s in range(2):
                    b = begin("bd", t, s)
                    end(group(b[0:m, :], [(gateT[:, c0:c0 + m], bd_rows[:, 512 * s:512 * s + 512])]), "bd", t, s)

            def tokens_turned():
                for k in range(8):
                    ins = turn(banks[k // 4][:, BLK * (k % 4):BLK * (k % 4) + BLK], xrow[:, 128 * k:128 * k + 128])
                ins.then_inc(m_gath, 1)

            pe.wait_ge(moe_tab, 1)
            taken(pe, "cnt")
            for t in range(3):
                taken(pe, "pos", t)
                for s in range(2):
                    taken(pe, "bd", t, s)
            nb = pe.value_load(nbi[0:1, 0:1].bitcast(I32), min_val=NE, max_val=MAXB)
            pe.wait_ge(m_xrow, 16)
            tokens_turned()
            with pe.Fori(0, nb) as b:
                pe.wait_ge(m_xg, b + 1)
                for c in range(4):
                    pe.wait_ge(chunk_in[c], 16 * b + 16)
                    w = up_w(c)
                    out = banks[2 + 2 * (c % 2) + c // 2]
                    for n in range(4):
                        for k in range(8):
                            ins = pe.matmul(out[:, BLK * n:BLK * n + BLK], w[:, k, 128 * n:128 * n + 128], xg[:, k, :],
                                            start=(k == 0), stop=(k == 7))
                    ins.then_inc(m_used, 1)
                pe.wait_ge(m_xrow, 16 * b + 32)
                tokens_turned()
                for c in range(2):
                    pe.wait_ge(m_hid, 2 * b + c + 1)
                    pe.wait_ge(chunk_in[4 + c], 16 * b + 16)
                    w = dn_w(c)
                    for k in range(4):
                        for n in range(2):
                            ins = pe.matmul(banks[6 + n][:, :], hid[:, 4 * c + k, :], w[:, k, 512 * n:512 * n + 512],
                                            start=(c == 0 and k == 0), stop=(c == 1 and k == 3),
                                            skip_group_check=True)
                    ins.then_inc(m_used, 1)

        @block.scalar
        def _(act):
            steps = [0]

            def step(ins):
                steps[0] += 1
                ins.then_inc(act_step, 1)
                act.wait_ge(act_step, steps[0])

            def take(ins, *name):
                n = JOB[name]
                ins.then_inc(bank_free[n % 8], 1)
                act.wait_ge(bank_free[n % 8], n // 8 + 1)

            def signal(ins, s, v):
                ins.then_inc(s, 1)
                act.wait_ge(s, v)

            def copy(out, src, scale=1.0):
                return act.activation(out, src, ACT.Copy, scale=scale)

            act.wait_ge(ld_x, 80)
            for t, (_, n) in enumerate(ROWS):
                signal(act.activation(xn_rows[0:n, t, :], x_rows[0:n, t, :], ACT.Square, accum_out=ss[0:n, t:t + 1]),
                       rms_s, t + 1)
            for t, (_, n) in enumerate(ROWS):
                act.wait_ge(rms_v, t + 1)
                signal(act.activation(ss[0:n, t:t + 1], ss[0:n, t:t + 1], ACT.Sqrt), rms_s, 4 + t)
            filled(act, "vecT")
            take(copy(vec[:, 0:NVEC], bank(("vecT",))[:, 0:NVEC]), "vecT")
            filled(act, "convT")
            take(copy(convst[:, :, :], bank(("convT",))[:, 0:48].rearrange("p (j c) -> p j c", j=3)), "convT")
            filled(act, "buT")
            take(copy(bu_t[:, :, :], bank(("buT",))[:, :].rearrange("p (c e) -> p c e", c=16)), "buT")
            for n in range(3):
                filled(act, "cq", n)
                signal(act.activation(sq[:, n, :], bank(("cq", n))[:, 0:NT], ACT.Square), cq_ready, n + 1)
                take(copy(cq[:, n, :], bank(("cq", n))[:, 0:NT], vec[:, V_GQ + n:V_GQ + n + 1]), "cq", n)
            for n in range(2):
                filled(act, "ckv", n)
                signal(act.activation(sq[:, 3 + n, :], bank(("ckv", n))[:, 0:NT], ACT.Square), cq_ready, n + 4)
                take(copy(lat[:, n, :], bank(("ckv", n))[:, 0:NT]), "ckv", n)
            filled(act, "kr")
            take(copy(kr_raw, bank(("kr",))[0:64, 0:NT]), "kr")
            for n, r in enumerate((rq, rk)):
                act.wait_ge(low_v, n + 1)
                signal(act.activation(r, r, ACT.Sqrt), low_s, n + 1)
            act.wait_ge(lg_d, 1)
            signal(act.activation(R_MX, R_A, ACT.Exp), lg_a, 1)
            act.wait_ge(lg_d, 2)
            signal(act.activation(R_MX, R_MX, ACT.Ln), lg_a, 2)
            act.wait_ge(gates_x, 1)
            step(act.activation(R_WI, R_WI, ACT.Exp, scale=-1.0))
            step(act.activation(R_DN, R_DN, ACT.Exp, scale=-1.0))
            signal(act.activation(R_WK, R_WK, ACT.Exp), gates4, 1)

            def sigmoid_qk(n):
                act.wait_ge(conv_done, n + 1)
                if n >= 2:
                    act.wait_ge(qk_ready, n - 1)
                signal(act.activation(sig[:, n % 2, :], qk[:, n, :], ACT.Sigmoid), sig_ready, n + 1)

            act.wait_ge(pad_set, 1)
            for n in range(16):
                if n == 8:
                    for t, (c0, m) in enumerate(KEYS):
                        filled(act, "kvrow", t)
                        take(copy(kvrow[0:m, t, :], bank(("kvrow", t))[0:m, 0:320]), "kvrow", t)
                filled(act, "qk", n)
                if n >= 2:
                    act.wait_ge(conv_done, n - 1)
                    act.wait_ge(tail_done, n - 1)
                p = bank(("qk", n))
                step(copy(u_pad[:, n % 2, 0:3], convst[:, :, n]))
                step(copy(u_pad[:, n % 2, 3:67], p[:, 0:64]))
                take(copy(u_pad[:, n % 2, 70:342], p[:, 64:NT]), "qk", n)
                if n:
                    sigmoid_qk(n - 1)
            sigmoid_qk(15)
            for h in range(4):
                filled(act, "wi", h)
                take(copy(wib[:, h, :], bank(("wi", h))[:, 0:NT]), "wi", h)
                step(copy(wprev[:, h, 0:1], wib[:, h, 63:64]))
                signal(copy(wprev[:, h, 1:6], wib[:, h, 79:NT:64]), wprev_ready, h + 1)
            for n in range(8):
                filled(act, "v", n)
                take(copy(vT[:, n, :], bank(("v", n))[:, 0:NT]), "v", n)
            filled(act, "convrow")
            take(copy(tailrow[:, :], bank(("convrow",))[0:96, 0:128]), "convrow")
            for n in range(8):
                filled(act, "o", n)
                take(act.activation(oT[:, n, :], bank(("o", n))[:, 0:NT], ACT.Sigmoid), "o", n)

            for h in range(4):
                taken(act, "mx", h)
            taken(act, "cols")
            for c, (c0, m) in enumerate(CHUNKS):
                if c:
                    taken(act, "s", c - 1)
                for h in range(4):
                    signal(act.activation(wexp[0:m, h, 0:m], emat[0:m, h, c0:c0 + m], ACT.Exp,
                                          bias=colT[0:m, c, 0, h:h + 1]), e_ready, 4 * c + h + 1)
                if c >= 2:
                    filled(act, "upd", c - 2, 7)
                for s in range(2):
                    filled(act, "krow", c, s)
                    p = bank(("krow", c, s))
                    h = 2 * s
                    step(copy(krow[0:m, c % 2, 256 * h:256 * h + 256], p[0:m, 0:256], colT[0:m, c, 2, h:h + 1]))
                    take(copy(krow[0:m, c % 2, 256 * h + 256:256 * h + 512], p[0:m, 256:512],
                              colT[0:m, c, 2, h + 1:h + 2]), "krow", c, s)
                for s in range(2):
                    filled(act, "vrow", c, s)
                    v = vrow[0:m, c % 2, :].rearrange("p (h e) -> p h e", h=4)[:, 2 * s:2 * s + 2, 0:256]
                    take(copy(v, bank(("vrow", c, s))[0:m, :].rearrange("p (h e) -> p h e", h=2)), "vrow", c, s)
                if c >= 2:
                    filled(act, "hT", c - 2)
                elif c == 1:
                    act.wait_ge(rows_zeroed, 16 * 17)
                for h in range(4):
                    filled(act, "num", c, h)
                    p = bank(("num", c, h))
                    step(act.activation(junk[0:m, 0:256], p[0:m, 0:256], ACT.Square, accum_out=hs[0:m, 0, h:h + 1]))
                    take(copy(num[0:m, c % 2, h, :], p[0:m, 0:257]), "num", c, h)
                act.wait_ge(hs_v, c + 1)
                signal(act.activation(hs[0:m, 4, :], hs[0:m, 3, :], ACT.Sqrt), hs_s, c + 1)
                if c in (0, 5):
                    filled(act, "nT", c)
                    take(copy(nrow[:, c // 5, :], bank(("nT", c))[0:8, 0:128]), "nT", c)

            for t in range(4):
                filled(act, "cacheT", t)
                p = bank(("cacheT", t))
                step(copy(cache_lat[:, :, 128 * t:128 * t + 128], p[:, 0:256].rearrange("p (r t) -> p r t", r=2)))
                take(copy(cache_kr[:, 128 * t:128 * t + 128], p[0:64, 256:384]), "cacheT", t)
            for hp in range(4):
                filled(act, "ukT", hp)
                take(copy(ukT[:, :, :], bank(("ukT", hp))[:, :].rearrange("p (h r) -> p h r", h=2)), "ukT", hp)
                for n in range(4):
                    filled(act, "ql", hp, n)
                    for j, (dst, src) in enumerate(by_chunk(qlat[:, n % 2, :], n // 2, bank(("ql", hp, n))[:, 0:NT])):
                        if j < 2:
                            step(copy(dst, src))
                        else:
                            take(copy(dst, src), "ql", hp, n)
                for c in range(7):
                    if c < 6:
                        u, m = 6 * hp + c, CHUNKS[c][1]
                        act.wait_ge(pmax, u + 1)
                        if u >= 2:
                            filled(act, "pT", (u - 2) // 6, (u - 2) % 6, 1 if (u - 2) % 6 == 0 else 0)
                        parts = [(0, PAST), (PAST, TS)] if c == 0 else [(0, CHUNKS[c][0] + m - TS)]
                        for p, (at, n) in enumerate(parts):
                            take(act.activation(prob[0:2 * m, u % 2, at:at + n], bank(("sc", hp, c, p))[0:2 * m, 0:n],
                                                ACT.Exp, bias=st[0:2 * m, u % 2, 3:4], scale=SCALE,
                                                accum_out=st[0:2 * m, u % 2, 4 + p:5 + p]), "sc", hp, c, p)
                    if c:
                        u, (c0, m) = 6 * hp + c - 1, CHUNKS[c - 1]
                        n = c0 + m - TS
                        if u >= 2:
                            filled(act, "ol", (u - 2) // 6, (u - 2) % 6)
                        filled(act, "pT", hp, c - 1, 0)
                        p = bank(("pT", hp, c - 1, 0))[:, :].rearrange("p (k q) -> p k q", k=4)
                        if c == 1:
                            take(copy(pT[:, u % 2, 0:4, :], p), "pT", hp, 0, 0)
                            filled(act, "pT", hp, 0, 1)
                            take(copy(pT[0:64, u % 2, 4, :], bank(("pT", hp, 0, 1))[0:64, 0:128]), "pT", hp, 0, 1)
                        else:
                            f, rest = n // 128, n % 128
                            if f:
                                step(copy(pT[:, u % 2, 0:f, 0:2 * m], p[:, 0:f, 0:2 * m]))
                            take(copy(pT[0:rest, u % 2, f, 0:2 * m], p[0:rest, f, 0:2 * m]), "pT", hp, c - 1, 0)
                for h in (0, 1):
                    filled(act, "ov", hp, h)
                    take(copy(ovT[:, 2 * hp + h, :], bank(("ov", hp, h))[:, 0:NT]), "ov", hp, h)
            for n in range(16):
                filled(act, "g", n)
                take(act.activation(gates[:, n, :], bank(("g", n))[:, 0:NT], ACT.Sigmoid), "g", n)

            for t, (_, n) in enumerate(ROWS):
                taken(act, "out", t, 0)
                taken(act, "out", t, 1)
                signal(act.activation(x2[0:n, t, :], x1[0:n, t, :], ACT.Square, accum_out=ss[0:n, 8 + t:9 + t]),
                       x1_ss, t + 1)
                act.wait_ge(x1_v, t + 1)
                signal(act.activation(ss[0:n, 8 + t:9 + t], ss[0:n, 8 + t:9 + t], ACT.Sqrt), x1_s, t + 1)
            for t, (c0, m) in enumerate(ROWS):
                for s in range(2):
                    filled(act, "x2T", t, s)
                    take(copy(x2T[:, 4 * s:4 * s + 4, c0:c0 + m],
                              bank(("x2T", t, s))[:, 0:4 * m].rearrange("p (k t) -> p k t", k=4)), "x2T", t, s)
            for t, (_, n) in enumerate(ROWS):
                act.wait_ge(gate_x, t + 1)
                signal(act.activation(gate[0:n, t, 0:4], gate[0:n, t, 0:4], ACT.Exp, accum_out=gsum[0:n, t:t + 1]),
                       gate_e, t + 1)

            act.wait_ge(moe_tab, 1)
            nb = act.value_load(nbi[0:1, 0:1].bitcast(I32), min_val=NE, max_val=MAXB)
            def tokens(n):
                return copy(xg[:, 4 * n:4 * n + 4, :], banks[n][:, :].rearrange("p (k s) -> p k s", k=4))

            act.wait_ge(m_gath, 1)
            step(tokens(0))
            signal(tokens(1), m_xg, 1)
            with act.Fori(0, nb) as b:
                for h in range(2):
                    act.wait_ge(m_gt, 2 * b + h + 1)
                    act.activation(sg[:, 4 * h:4 * h + 4, :], gt[:, 4 * h:4 * h + 4, :], ACT.Sigmoid, scale=ALPHA
                                   ).then_inc(m_sig, 1)
                    act.wait_ge(m_sig, 2 * b + h + 1)
                act.wait_ge(m_gath, b + 2)
                tokens(0).then_inc(m_act, 1)
                act.wait_ge(m_act, 2 * b + 1)
                tokens(1).then_inc(m_xg, 1)
                act.wait_ge(m_used, 6 * b + 6)
                act.wait_ge(yrow_free, b + 1)
                act.wait_ge(m_xg, b + 2)
                copy(yrow[:, 0:512], banks[6][:, :]).then_inc(m_act, 1)
                act.wait_ge(m_act, 2 * b + 2)
                copy(yrow[:, 512:1024], banks[7][:, :]).then_inc(m_yrow, 1)
                act.wait_ge(m_yrow, b + 1)
                act.wait_ge(moe_tab, 1)
                act.nop()

            for t, (_, n) in enumerate(ROWS):
                act.wait_ge(fin_v, 2 * t + 1)
                signal(act.activation(x2[0:n, t, :], x1[0:n, t, :], ACT.Square, accum_out=ss[0:n, 12 + t:13 + t]),
                       fin_ss, t + 1)
                act.wait_ge(fin_v, 2 * t + 2)
                signal(act.activation(ss[0:n, 12 + t:13 + t], ss[0:n, 12 + t:13 + t], ACT.Sqrt), fin_s, t + 1)

        @block.vector
        def _(dve):
            steps = [0]

            def step(ins):
                steps[0] += 1
                ins.then_inc(dve_step, 1)
                dve.wait_ge(dve_step, steps[0])

            def take(ins, *name):
                n = JOB[name]
                ins.then_inc(bank_free[n % 8], 1)
                dve.wait_ge(bank_free[n % 8], n // 8 + 1)

            def signal(ins, s, v):
                ins.then_inc(s, 1)
                dve.wait_ge(s, v)

            def ts(out, a, s1, op0, s2=None, op1=ALU.bypass):
                return dve.tensor_scalar(out, a, s1, s2, op0, op1)

            def tt(out, a, b, op):
                return dve.tensor_tensor(out, a, b, op)

            def stt(out, a, s, b, op0, op1):
                return dve.scalar_tensor_tensor(out=out, in0=a, scalar=s, in1=b, op0=op0, op1=op1)

            dve.wait_ge(ld_x, 80)
            for t, (_, n) in enumerate(ROWS):
                dve.wait_ge(rms_s, 3)
                signal(ts(ss[0:n, t:t + 1], ss[0:n, t:t + 1], 1.0 / D, ALU.mult, EPS, ALU.add), rms_v, t + 1)
            for t, (_, n) in enumerate(ROWS):
                dve.wait_ge(rms_s, 4 + t)
                step(dve.reciprocal(ss[0:n, t:t + 1], ss[0:n, t:t + 1]))
                signal(ts(xn_rows[0:n, t, :], x_rows[0:n, t, :], ss[0:n, t:t + 1], ALU.mult), xn_ready, t + 1)
            taken(dve, "vecT")
            for t, (c0, m) in enumerate(ROWS):
                for s in range(2):
                    filled(dve, "xT", t, s)
                    g = vec[:, V_GMIX + 4 * s:V_GMIX + 4 * s + 4].unsqueeze(2).broadcast_to([128, 4, m])
                    take(tt(xT[:, 4 * s:4 * s + 4, c0:c0 + m],
                            bank(("xT", t, s))[:, 0:4 * m].rearrange("p (k t) -> p k t", k=4), g, ALU.mult),
                         "xT", t, s)
            dve.wait_ge(ld_mem, 64)
            step(dve.memset(mst[:, 1:2], 0.0))
            signal(dve.tensor_copy(C[:, :, 256], vec[:, V_N0:V_N0 + 8]), n_set, 1)
            filled(dve, "ig")
            take(ts(R_IG, bank(("ig",))[0:4, 0:NT], b_if[:, 0:1], ALU.add), "ig")
            filled(dve, "fg")
            take(ts(R_LF, bank(("fg",))[0:4, 0:NT], b_if[:, 1:2], ALU.add), "fg")
            for n, (name, r, w) in enumerate((("ssq", rq, QL), ("ssk", rk, KVL))):
                filled(dve, name)
                ins = ts(r, bank((name,))[:, 0:NT], 1.0 / w, ALU.mult, EPS, ALU.add)
                take(ins, name)
                signal(ts(ss[:, 15:16], r[:, 0:1], 1.0, ALU.mult), low_v, n + 1)
            filled(dve, "krs")
            take(tt(kr_tmp, bank(("krs",))[0:64, 0:NT], cst("sin", 64), ALU.mult), "krs")
            step(tt(krT, kr_raw, cst("cos", 64), ALU.mult))
            signal(tt(krT, krT, kr_tmp, ALU.add), kr_ready, 1)
            for n, r in enumerate((rq, rk)):
                dve.wait_ge(low_s, n + 1)
                step(dve.reciprocal(r, r))
            for n in range(2):
                signal(stt(lat[:, n, :], lat[:, n, :], vec[:, V_GKV + n:V_GKV + n + 1], rk, ALU.mult, ALU.mult),
                       kv_ready, n + 1)
            step(ts(R_B, R_LF, 0.0, ALU.min))
            step(ts(R_A, R_LF, 0.0, ALU.max))
            signal(tt(R_A, R_B, R_A, ALU.subtract), lg_d, 1)
            dve.wait_ge(lg_a, 1)
            signal(ts(R_MX, R_MX, 1.0, ALU.add), lg_d, 2)
            dve.wait_ge(lg_a, 2)
            step(tt(R_LF, R_B, R_MX, ALU.subtract))
            for c0, m in CHUNKS:
                s = slice(c0, c0 + m)
                step(dve.tensor_tensor_scan(R_B[:, s], cst("ones", 4)[:, 0:m], R_LF[:, s], 0.0, ALU.mult, ALU.add))
            step(tt(R_A, R_IG, R_B, ALU.subtract))
            for c, (c0, m) in enumerate(CHUNKS):
                s, e = slice(c0, c0 + m), slice(c0 + m - 1, c0 + m)
                step(dve.tensor_tensor_scan(R_MX[:, s], R_A[:, s], R_A[:, s], mst[:, c:c + 1], ALU.max, ALU.max))
                new = 8 if c == 0 else c + 1
                step(tt(mst[:, new:new + 1], R_B[:, e], R_MX[:, e], ALU.add))
                step(ts(R_WI[:, s], R_MX[:, s], mst[:, c:c + 1], ALU.subtract))
                step(ts(R_WK[:, s], R_A[:, s], R_MX[:, e], ALU.subtract))
            signal(tt(R_DN, R_B, R_MX, ALU.add), gates_x, 1)

            def silu(n):
                dve.wait_ge(sig_ready, n + 1)
                signal(stt(qk[:, n, :], qk[:, n, :], 1.0 if n < 8 else 1.0 / 16, sig[:, n % 2, :],
                           ALU.mult, ALU.mult), qk_ready, n + 1)

            for n in range(16):
                taken(dve, "qk", n)
                u = u_pad[:, n % 2, :]

                def w(j):
                    return vec[:, V_WCONV + 16 * j + n:V_WCONV + 16 * j + n + 1]

                step(ts(qk[:, n, :], u[:, 0:339], w(0), ALU.mult, vec[:, V_BCONV + n:V_BCONV + n + 1], ALU.add))
                for j in (1, 2):
                    step(stt(qk[:, n, :], u[:, j:j + 339], w(j), qk[:, n, :], ALU.mult, ALU.add))
                signal(stt(qk[:, n, :], u[:, 3:342], w(3), qk[:, n, :], ALU.mult, ALU.add), conv_done, n + 1)
                if n:
                    silu(n - 1)
            silu(15)
            for h in range(4):
                filled(dve, "mx", h)
                take(stt(emat[:, h, :], bank(("mx", h))[0:64, 0:NT], -1.0, cst("mask", 64), ALU.mult, ALU.add),
                     "mx", h)
            filled(dve, "cols")
            p = bank(("cols",))
            step(dve.tensor_copy(colT[:, 0, :, :], p[0:64, 0:12].rearrange("p (a b) -> p a b", a=3)))
            step(dve.tensor_copy(colT[0:16, 1, :, :], p[0:16, 12:24].rearrange("p (a b) -> p a b", a=3)))
            take(dve.tensor_copy(colT[:, 2:6, :, :], p[0:64, 24:72].rearrange("p (c a b) -> p c a b", c=4, a=3)),
                 "cols")
            for n in range(8):
                taken(dve, "o", n)
                step(ts(oT[:, n, :], oT[:, n, :], vec[:, V_GMH + n:V_GMH + n + 1], ALU.mult))

            def heads_out(c):
                c0, m = CHUNKS[c]
                filled(dve, "hT", c)
                take(tt(oT[:, :, c0:c0 + m],
                        bank(("hT", c))[:, :].rearrange("p (k t) -> p k t", k=8)[:, :, 0:m],
                        oT[:, :, c0:c0 + m], ALU.mult), "hT", c)

            dve.wait_ge(wprev_ready, 4)
            for c, (c0, m) in enumerate(CHUNKS):
                q0 = qcol(c0)
                if c:
                    filled(dve, "num", c - 1, 3)
                dve.wait_ge(e_ready, 4 * c + 4)
                filled(dve, "s", c)
                take(tt(sT[0:m, :, 0:m], bank(("s", c))[0:m, 0:256].rearrange("p (h l) -> p h l", h=4)[:, :, 0:m],
                        wexp[0:m, :, 0:m], ALU.mult), "s", c)
                for h in range(4):
                    q = qk[:, 2 * h:2 * h + 2, q0:q0 + m]
                    ins = tt(q, q, wib[:, h:h + 1, c0:c0 + m].broadcast_to([128, 2, m]), ALU.mult)
                    if h < 3:
                        step(ins)
                    else:
                        signal(ins, q_scaled, c + 1)
                for h in range(4):
                    taken(dve, "num", c, h)
                qn_ = num[0:m, c % 2, :, 256]
                step(stt(hs[0:m, 1, :], qn_, -1.0, qn_, ALU.mult, ALU.max))
                step(tt(hs[0:m, 1, :], hs[0:m, 1, :], colT[0:m, c, 1, :], ALU.max))
                step(dve.reciprocal(hs[0:m, 2, :], hs[0:m, 1, :]))
                step(tt(hs[0:m, 3, :], hs[0:m, 2, :], hs[0:m, 2, :], ALU.mult))
                step(tt(hs[0:m, 3, :], hs[0:m, 3, :], hs[0:m, 0, :], ALU.mult))
                signal(ts(hs[0:m, 3, :], hs[0:m, 3, :], 1.0 / 256, ALU.mult, EPS, ALU.add), hs_v, c + 1)
                if c == 1:
                    dve.wait_ge(stored_c, 16)
                    filled(dve, "nT", 0)
                for n in range(8):
                    filled(dve, "upd", c, n)
                    p = bank(("upd", c, n))[:, 0:257]
                    if c == 1:
                        take(dve.tensor_copy(C[:, n, :], p), "upd", c, n)
                    else:
                        take(stt(C[:, n, :], C[:, n, :], wprev[:, n // 2, c:c + 1], p, ALU.mult, ALU.add),
                             "upd", c, n)
                dve.wait_ge(hs_s, c + 1)
                step(dve.reciprocal(hs[0:m, 5, :], hs[0:m, 4, :]))
                step(tt(hs[0:m, 5, :], hs[0:m, 5, :], hs[0:m, 2, :], ALU.mult))
                for h in range(4):
                    ins = ts(num[0:m, c % 2, h, 0:256], num[0:m, c % 2, h, 0:256], hs[0:m, 5, h:h + 1], ALU.mult)
                    if h < 3:
                        step(ins)
                    else:
                        signal(ins, hn_ready, c + 1)
                if c:
                    heads_out(c - 1)
            heads_out(5)

            for hp in range(4):
                for h in (0, 1):
                    filled(dve, "qn", hp, h)
                    take(tt(qn[:, h, :], bank(("qn", hp, h))[:, 0:NT], rq, ALU.mult), "qn", hp, h)
                    filled(dve, "qr", hp, h)
                    take(tt(qx[:, h, :], bank(("qr", hp, h))[0:64, 0:NT], rq[0:64, :], ALU.mult), "qr", hp, h)
                    filled(dve, "qrs", hp, h)
                    take(tt(qtmp, bank(("qrs", hp, h))[0:64, 0:NT], cst("sin", 64), ALU.mult), "qrs", hp, h)
                    step(tt(qx[:, h, :], qx[:, h, :], cst("cos", 64), ALU.mult))
                    for j, ((dst, a), (_, b)) in enumerate(zip(by_chunk(qr, h, qx[:, h, :]), by_chunk(qr, h, qtmp))):
                        ins = tt(dst, a, b, ALU.add)
                        if j < 2:
                            step(ins)
                        else:
                            signal(ins, q_ready, 2 * hp + h + 1)
                for c in range(8):
                    if c < 6:
                        u, m = 6 * hp + c, CHUNKS[c][1]
                        s = st[0:2 * m, u % 2, :]
                        parts = [PAST, TS] if c == 0 else [CHUNKS[c][0] + m - TS]
                        for p, n in enumerate(parts):
                            filled(dve, "sc", hp, c, p)
                            step(dve.tensor_reduce(s[:, p:p + 1], bank(("sc", hp, c, p))[0:2 * m, 0:n], AX.X, ALU.max))
                        if c == 0:
                            step(tt(s[:, 0:1], s[:, 0:1], s[:, 1:2], ALU.max))
                        signal(ts(s[:, 3:4], s[:, 0:1], -SCALE, ALU.mult), pmax, u + 1)
                    if 1 <= c <= 6:
                        u, (c0, m) = 6 * hp + c - 1, CHUNKS[c - 1]
                        n = PAST + TS if c == 1 else c0 + m - TS
                        s = st[0:2 * m, u % 2, :]
                        for p in range(2 if c == 1 else 1):
                            taken(dve, "sc", hp, c - 1, p)
                        if c == 1:
                            step(tt(s[:, 4:5], s[:, 4:5], s[:, 5:6], ALU.add))
                        step(dve.reciprocal(s[:, 6:7], s[:, 4:5]))
                        signal(ts(prob[0:2 * m, u % 2, 0:n], prob[0:2 * m, u % 2, 0:n], s[:, 6:7], ALU.mult),
                               pnorm, u + 1)
                    if c >= 2:
                        c0, m = CHUNKS[c - 2]
                        filled(dve, "ol", hp, c - 2)
                        p = bank(("ol", hp, c - 2))[:, 0:256].rearrange("p (r q) -> p r q", r=2)[:, :, 0:2 * m]
                        for r in (0, 1):
                            ins = dve.tensor_copy(olat[:, r, :, c0:c0 + m],
                                                  p[:, r, :].rearrange("p (h t) -> p h t", h=2))
                            if r:
                                take(ins, "ol", hp, c - 2)
                            else:
                                step(ins)
            for n in range(8):
                taken(dve, "g", n)
                filled(dve, "ya", n)
                take(tt(mixed[:, n, :], bank(("ya", n))[:, 0:NT], gates[:, n, :], ALU.mult), "ya", n)
            for n in range(8):
                taken(dve, "g", 8 + n)
                filled(dve, "yb", n)
                take(tt(sig[:, 0, 0:NT], bank(("yb", n))[:, 0:NT], gates[:, 8 + n, :], ALU.mult), "yb", n)
                signal(tt(mixed[:, n, :], mixed[:, n, :], sig[:, 0, 0:NT], ALU.add), mix_a, n + 1)
            dve.wait_ge(ld_x1, 80)
            for t, (_, m) in enumerate(ROWS):
                for s in range(2):
                    filled(dve, "out", t, s)
                    x = x1[0:m, t, 512 * s:512 * s + 512]
                    take(tt(x, bank(("out", t, s))[0:m, :], x, ALU.add), "out", t, s)
            dve.wait_ge(ld_late, 64)
            for t, (_, m) in enumerate(ROWS):
                r = ss[0:m, 8 + t:9 + t]
                dve.wait_ge(x1_ss, t + 1)
                signal(ts(r, r, 1.0 / D, ALU.mult, EPS, ALU.add), x1_v, t + 1)
                dve.wait_ge(x1_s, t + 1)
                step(dve.reciprocal(r, r))
                signal(stt(x2[0:m, t, :], x1[0:m, t, :], r, g_ffn_b[0:m, :], ALU.mult, ALU.mult), x2_ready, t + 1)

            for t, (_, m) in enumerate(ROWS):
                filled(dve, "lg", t)
                take(tt(logit[0:m, t, :], bank(("lg", t))[0:m, 0:NE], b_router_b[0:m, :], ALU.add), "lg", t)
                step(dve.max(top[0:m, t, :], logit[0:m, t, :]))
                step(dve.max_index(topi[0:m, t, :].bitcast(U32), top[0:m, t, :], logit[0:m, t, :]))
                step(dve.tensor_copy(topif[0:m, t, :], topi[0:m, t, :].bitcast(U32)))
                for k in range(4):
                    step(ts(onehot[0:m, t, k, :], cst("expert")[0:m, :], topif[0:m, t, k:k + 1], ALU.is_equal))
                c = chosen[0:m, t, :]
                step(tt(c, onehot[0:m, t, 0, :], onehot[0:m, t, 1, :], ALU.add))
                step(tt(c, c, onehot[0:m, t, 2, :], ALU.add))
                signal(tt(c, c, onehot[0:m, t, 3, :], ALU.add), chosen_set, t + 1)
                signal(ts(gate[0:m, t, 0:4], top[0:m, t, 0:4], top[0:m, t, 0:1], ALU.subtract), gate_x, t + 1)
            for t, (_, m) in enumerate(ROWS):
                filled(dve, "pos", t)
                take(dve.tensor_copy(posm[0:m, t, :], bank(("pos", t))[0:m, 0:NE]), "pos", t)
            filled(dve, "cnt")
            cnt = bank(("cnt",))[:, 0:NE]
            step(ts(nblk, cnt, float(BLK), ALU.is_gt, 1.0, ALU.add))
            more = range(2 * BLK, NT, BLK)
            for n in more:
                ins = stt(nblk, cnt, float(n), nblk, ALU.is_gt, ALU.add)
                if n == more[-1]:
                    take(ins, "cnt")
                else:
                    step(ins)
            step(dve.tensor_tensor_scan(pend, cst("ones")[:, 0:NE], nblk, 0.0, ALU.mult, ALU.add))
            step(tt(start, pend, nblk, ALU.subtract))
            for t, (_, m) in enumerate(ROWS):
                step(stt(posm[0:m, t, :], start[0:m, :], float(BLK), posm[0:m, t, :], ALU.mult, ALU.add))
                for k in range(4):
                    step(dve.tensor_tensor_reduce(t32[0:m, :], onehot[0:m, t, k, :], posm[0:m, t, :], 1.0, 0.0,
                                                  ALU.mult, ALU.add, dest[0:m, t, k:k + 1]))
                signal(dve.tensor_copy(desti[0:m, t, :].bitcast(U32), dest[0:m, t, :]), desti_set, t + 1)
            cmp = r_o[0:1, 0:NB1 * NE].rearrange("p (b e) -> p b e", e=NE)
            step(tt(cmp, cst("block", 1).unsqueeze(2).broadcast_to([1, NB1, NE]),
                    pend[0:1, :].unsqueeze(1).broadcast_to([1, NB1, NE]), ALU.is_ge))
            step(dve.tensor_reduce(be[0:1, :], cmp, AX.X, ALU.add))
            step(ts(be[0:1, :], be[0:1, :], float(NE - 1), ALU.min))
            step(dve.tensor_copy(bei[0:1, :].bitcast(I32), be[0:1, :]))
            signal(dve.tensor_copy(nbi[0:1, 0:1].bitcast(I32), pend[0:1, NE - 1:NE]), moe_tab, 1)
            for t, (_, m) in enumerate(ROWS):
                dve.wait_ge(gate_e, t + 1)
                step(dve.reciprocal(gsum[0:m, t:t + 1], gsum[0:m, t:t + 1]))
                step(ts(gate[0:m, t, 0:4], gate[0:m, t, 0:4], gsum[0:m, t:t + 1], ALU.mult))
                g = gmat[0:m, t, :]
                step(ts(g, onehot[0:m, t, 0, :], gate[0:m, t, 0:1], ALU.mult))
                for k in (1, 2, 3):
                    ins = stt(g, onehot[0:m, t, k, :], gate[0:m, t, k:k + 1], g, ALU.mult, ALU.add)
                    if k < 3:
                        step(ins)
                    else:
                        signal(ins, gates_set, t + 1)
            for t, (c0, m) in enumerate(ROWS):
                filled(dve, "gT", t)
                take(dve.tensor_copy(gateT[:, c0:c0 + m], bank(("gT", t))[0:NE, 0:m]), "gT", t)
            for t, (_, m) in enumerate(ROWS):
                for s in range(2):
                    filled(dve, "bd", t, s)
                    x = x1[0:m, t, 512 * s:512 * s + 512]
                    take(tt(x, bank(("bd", t, s))[0:m, :], x, ALU.add), "bd", t, s)
            dve.wait_ge(stored, 16 * 14)

            nb = dve.value_load(nbi[0:1, 0:1].bitcast(I32), min_val=NE, max_val=MAXB)
            dve.wait_ge(moe_tab, 1)
            with dve.Fori(0, nb) as b:
                e = dve.value_load(bei[0:1, bass.ds(b, 1)].bitcast(I32), min_val=0, max_val=NE - 1)
                bias = [bu_t[:, 4 * n:4 * n + 4, bass.ds(e, 1)].broadcast_to([128, 4, BLK]) for n in range(4)]

                def order(ins, n):
                    ins.then_inc(m_dve, 1)
                    dve.wait_ge(m_dve, 6 * b + n)

                def blk(n):
                    return banks[n][:, :].rearrange("p (k s) -> p k s", k=4)

                for h in range(2):
                    g, u, q = gt[:, 4 * h:4 * h + 4, :], up[:, 4 * h:4 * h + 4, :], sg[:, 4 * h:4 * h + 4, :]
                    dve.wait_ge(m_used, 6 * b + 2 * h + 1)
                    order(tt(g, blk(2 + h), bias[h], ALU.add), 3 * h + 1)
                    ts(g, g, LIMIT, ALU.min).then_inc(m_gt, 1)
                    dve.wait_ge(m_gt, 2 * b + h + 1)
                    dve.wait_ge(m_used, 6 * b + 2 * h + 2)
                    order(tt(u, blk(4 + h), bias[2 + h], ALU.add), 3 * h + 2)
                    order(ts(u, u, LIMIT, ALU.min, -LIMIT, ALU.max), 3 * h + 3)
                    dve.wait_ge(m_sig, 2 * b + h + 1)
                    tt(g, g, q, ALU.mult).then_inc(m_glu, 1)
                    dve.wait_ge(m_glu, 2 * b + h + 1)
                    stt(hid[:, 4 * h:4 * h + 4, :], u, 1.0, g, ALU.add, ALU.mult).then_inc(m_hid, 1)
                    dve.wait_ge(m_hid, 2 * b + h + 1)
                dve.wait_ge(moe_tab, 1)
                dve.nop()

            for t, (_, m) in enumerate(ROWS):
                dve.wait_ge(fin_y[t], 64)
                for k in range(4):
                    y = ring[0:m, (4 * t + k) * D:(4 * t + k + 1) * D]
                    ins = stt(x1[0:m, t, :], y, gate[0:m, t, k:k + 1], x1[0:m, t, :], ALU.mult, ALU.add)
                    if k < 3:
                        step(ins)
                    else:
                        signal(ins, fin_v, 2 * t + 1)
                r = ss[0:m, 12 + t:13 + t]
                dve.wait_ge(fin_ss, t + 1)
                signal(ts(r, r, 1.0 / D, ALU.mult, EPS, ALU.add), fin_v, 2 * t + 2)
                dve.wait_ge(fin_s, t + 1)
                step(dve.reciprocal(r, r))
                signal(stt(x1[0:m, t, :], x1[0:m, t, :], r, g_fin_b[0:m, :], ALU.mult, ALU.mult), fin_out, t + 1)

        @block.gpsimd
        def _(pool):
            pool.memset(u_pad[:, :, 67:70], 0.0).then_inc(pad_set, 1)
            zero = r_c[0:BLK, 3084:3084 + D]
            pool.memset(zero, 0.0).then_inc(zero_set, 1)
            pool.wait_ge(zero_set, 1)
            pool.dma_start(y_rows_dram[NE * BLK:MAXB * BLK, :].rearrange("(b s) d -> s b d", s=BLK),
                           zero.unsqueeze(1).broadcast_to([BLK, MAXB - NE, D])).then_inc(rows_zeroed, 16)
            filled(pool, "xT", 2, 1)
            ones = vrow.rearrange("p c (h e) -> p c h e", h=4)[:, :, :, 256]
            pool.memset(ones, 1.0).then_inc(ones_set, 1)
            for n in range(16):
                b0, b1 = (MAXB + 1) * n // 16, (MAXB + 1) * (n + 1) // 16
                pool.dma_start(x_rows_dram[b0 * BLK:b1 * BLK, :].rearrange("(b s) d -> s b d", s=BLK),
                               zero.unsqueeze(1).broadcast_to([BLK, b1 - b0, D])).then_inc(rows_zeroed, 16)
                taken(pool, "qk", n)
                pool.tensor_copy(tail[:, 0, :, n], u_pad[:, n % 2, 64:67])
                pool.tensor_copy(tail[:, 1, :, n], u_pad[:, n % 2, 339:342]).then_inc(tail_done, 1)

            def store(dst, src, s=stored):
                pool.dma_start(dst, src).then_inc(s, 16)

            for t, (c0, m) in enumerate(KEYS):
                taken(pool, "kvrow", t)
                if t < 3:
                    store(o["p_lat"][0, 0, c0 - TS:c0 - TS + m, :], kvrow[0:m, t, 0:256])
                    store(o["p_kr"][0, 0, c0 - TS:c0 - TS + m, :], kvrow[0:m, t, 256:320])
                else:
                    store(o["s_lat"][0, 0], kvrow[0:m, t, 0:256])
                    store(o["s_kr"][0, 0], kvrow[0:m, t, 256:320])
            taken(pool, "convrow")
            for w, name in enumerate(("s_conv", "p_conv")):
                store(o[name][0, 0].rearrange("j (c p) -> (j c) p", p=128), tailrow[48 * w:48 * w + 48, :])
            pool.wait_ge(gates_x, 1)
            for w, name in enumerate(("s_m", "p_m")):
                pool.dma_start(o[name][0].rearrange("b h -> h b"), mst[:, 8 - 2 * w:9 - 2 * w],
                               allow_slow_non_contiguous=True).then_inc(stored, 16)
            for c, w in ((0, "s"), (5, "p")):
                for n in range(8):
                    taken(pool, "upd", c, n)
                store(o[w + "_C"][0, 0].rearrange("h (b p) e -> p (h b) e", p=128), C[:, :, 0:256], stored_c)
                taken(pool, "nT", c)
                store(o[w + "_n"][0, 0].rearrange("h (b p) -> (h b) p", p=128), nrow[:, c // 5, :])

            pool.wait_ge(rows_zeroed, 16 * 17)
            for t, (_, m) in enumerate(ROWS):
                pool.wait_ge(desti_set, t + 1)
                for k in range(4):
                    pool.indirect_dma_start(
                        x_rows_dram[:, :], bass.IndirectOffsetOnAxis(ap=desti[0:m, t, k:k + 1].bitcast(U32), axis=0),
                        x2[0:m, t, :], None).then_inc(x_sent, 16)
            pool.wait_ge(moe_tab, 1)
            nb = pool.value_load(nbi[0:1, 0:1].bitcast(I32), min_val=NE, max_val=MAXB)
            pool.sem_inc(yrow_free, 1)
            with pool.Fori(0, nb) as b:
                dst = y_rows_dram[bass.ds(pool.snap(b * BLK), BLK), :]
                pool.wait_ge(m_yrow, b + 1)
                pool.wait_ge(moe_tab, 1)
                pool.dma_start(dst, yrow).then_inc(m_store, 16)
                pool.wait_ge(m_store, 16 * b + 16)
                pool.sem_inc(yrow_free, 1)
            pool.wait_ge(m_store, 16 * nb)
            word = u_pad[0:1, 0, 67:68]
            pool.tensor_tensor(word, word, word, ALU.add).then_inc(blocks_out, 1)
            pool.wait_ge(blocks_out, 1)
            for t, (_, m) in enumerate(ROWS):
                for k in range(4):
                    pool.indirect_dma_start(
                        ring[0:m, (4 * t + k) * D:(4 * t + k + 1) * D], None, y_rows_dram[:, :],
                        bass.IndirectOffsetOnAxis(ap=desti[0:m, t, k:k + 1].bitcast(U32), axis=0)
                    ).then_inc(fin_y[t], 16)
            for t in range(3):
                pool.wait_ge(fin_out, t + 1)
                if t == 0:
                    store(o["y_s"][0], x1[0:64, 0, :])
                    store(o["y_p"][0, 0:48, :], x1[80:128, 0, :])
                elif t == 1:
                    store(o["y_p"][0, 48:176, :], x1[:, 1, :])
                else:
                    store(o["y_p"][0, 176:256, :], x1[0:80, 2, :])
            pool.wait_ge(stored, 16 * 18)
            pool.wait_ge(stored_c, 32)
            pool.wait_ge(x_sent, 16 * 12)


INS = ["x_prompt", "x_sample", "cache_kv_latent", "cache_k_rope", "state_mlstm_C", "state_mlstm_n", "state_mlstm_m",
       "state_conv", "meta_tokens", "g_mix_norm", "w_in", "b_if", "w_conv", "b_conv", "g_mh_norm", "w_proj_a",
       "g_q_norm", "g_kv_norm", "w_uq", "w_uk", "w_uv", "w_proj_b", "w_out", "g_ffn_norm", "w_router", "b_router",
       "w_gate_up", "b_gate_up", "w_down", "b_down", "g_final_norm"]
OUTS = [("y_p", (1, TX, D)), ("y_s", (1, TS, D)), ("p_lat", (1, 1, TP, KVL)), ("p_kr", (1, 1, TP, ROPE)),
        ("p_C", (1, 1, 4, 256, 256)), ("p_n", (1, 1, 4, 256)), ("p_m", (1, 1, 4)), ("p_conv", (1, 1, 3, 2048)),
        ("s_lat", (1, 1, TS, KVL)), ("s_kr", (1, 1, TS, ROPE)), ("s_C", (1, 1, 4, 256, 256)), ("s_n", (1, 1, 4, 256)),
        ("s_m", (1, 1, 4)), ("s_conv", (1, 1, 3, 2048))]


def kernel(**inputs):
    import concourse.bacc as bacc
    from concourse.bass_utils import run_bass_kernel_spmd as run

    nc = bacc.Bacc("TRN2", target_bir_lowering=False, num_devices=1)
    arrays, i, o = {}, {}, {}
    for name in INS:
        arrays["in_" + name] = np.ascontiguousarray(inputs[name])
    arrays["in_consts"] = constants()
    for name, a in arrays.items():
        i[name[3:]] = nc.dram_tensor(name, a.shape, F32, kind="ExternalInput").ap()
    for name, shape in OUTS:
        o[name] = nc.dram_tensor("out_" + name, shape, F32, kind="ExternalOutput").ap()
    x_rows_dram = nc.dram_tensor("x_rows", ((MAXB + 1) * BLK, D), F32).ap()
    y_rows_dram = nc.dram_tensor("y_rows", (MAXB * BLK, D), F32).ap()
    build(nc, i, o, x_rows_dram, y_rows_dram)
    r = run(nc, [arrays], core_ids=[0])
    return tuple(r.results[0]["out_" + name] for name, _ in OUTS)
```
